# Optimizing a Trainium2 kernel written in Bass

```python
import math
import jax, jax.numpy as jnp
from jax import lax
import numpy as np

D_MODEL = 1024
BATCH = 1
SEQ = 256
DEPTH = 1

N_META = 16
D_SSM = D_MODEL // 2
SSM_GROUP = 16
N_SSM_GROUPS = D_SSM // SSM_GROUP
SSM_STATE = 64
D_CONV = D_MODEL // 2
CONV_WIDTH = 31
N_EXPERTS = 32
TOP_K = 4
D_EXPERT = D_MODEL
SWIGLU_LIMIT = 7.0
SWIGLU_ALPHA = 1.702
RMS_EPS = 1e-6
LN_EPS = 1e-5
DT_MIN = 1e-3
DT_MAX = 1e-1
D_IN_PROJ = D_SSM + 2 * D_CONV + 2 * D_MODEL

kernel_name = "hybrid_s5_conformer_moe_block"

def _rmsnorm(x, g):
    xf = x.astype(jnp.float32)
    y = xf * lax.rsqrt(jnp.mean(xf * xf, axis=-1, keepdims=True) + RMS_EPS)
    return (y * g.astype(jnp.float32)).astype(x.dtype)

def _layernorm(x, g, b):
    xf = x.astype(jnp.float32)
    mu = jnp.mean(xf, axis=-1, keepdims=True)
    var = jnp.mean(jnp.square(xf - mu), axis=-1, keepdims=True)
    y = (xf - mu) * lax.rsqrt(var + LN_EPS)
    return (y * g.astype(jnp.float32) + b.astype(jnp.float32)).astype(x.dtype)

def _ssm_combine(left, right):
    ar_i, ai_i, br_i, bi_i = left
    ar_j, ai_j, br_j, bi_j = right
    return (ar_j * ar_i - ai_j * ai_i,
            ar_j * ai_i + ai_j * ar_i,
            ar_j * br_i - ai_j * bi_i + br_j,
            ar_j * bi_i + ai_j * br_i + bi_j)

def _s5_branch(u, a_re, a_im, log_dt, b_re, b_im, c_re, c_im, d_skip):
    bsz, seq_len, _ = u.shape
    uf = u.astype(jnp.float32).reshape(bsz, seq_len, N_SSM_GROUPS, SSM_GROUP)
    a_re = a_re.astype(jnp.float32)
    a_im = a_im.astype(jnp.float32)
    dt = jnp.exp(log_dt.astype(jnp.float32))[:, None]
    decay = jnp.exp(a_re * dt)
    abar_re = decay * jnp.cos(a_im * dt)
    abar_im = decay * jnp.sin(a_im * dt)
    den = a_re * a_re + a_im * a_im
    nr = abar_re - 1.0
    coef_re = (nr * a_re + abar_im * a_im) / den
    coef_im = (abar_im * a_re - nr * a_im) / den
    bu_re = jnp.einsum('blgh,gph->lbgp', uf, b_re.astype(jnp.float32))
    bu_im = jnp.einsum('blgh,gph->lbgp', uf, b_im.astype(jnp.float32))
    drive_re = coef_re * bu_re - coef_im * bu_im
    drive_im = coef_re * bu_im + coef_im * bu_re
    ar = jnp.broadcast_to(abar_re, (seq_len, 1, N_SSM_GROUPS, SSM_STATE))
    ai = jnp.broadcast_to(abar_im, (seq_len, 1, N_SSM_GROUPS, SSM_STATE))
    _, _, s_re, s_im = lax.associative_scan(_ssm_combine, (ar, ai, drive_re, drive_im), axis=0)
    y = (jnp.einsum('lbgp,ghp->blgh', s_re, c_re.astype(jnp.float32))
         - jnp.einsum('lbgp,ghp->blgh', s_im, c_im.astype(jnp.float32)))
    y = y.reshape(bsz, seq_len, D_SSM) + d_skip.astype(jnp.float32) * u.astype(jnp.float32)
    return y.astype(u.dtype)

def _conformer_branch(conv_in, dw_w, dw_b, ln_g, ln_b, w_conv_out):
    val, gate = jnp.split(conv_in, 2, axis=-1)
    c = val * jax.nn.sigmoid(gate)
    c = lax.conv_general_dilated(
        c, dw_w.astype(c.dtype), window_strides=(1,), padding=[(CONV_WIDTH - 1, 0)],
        dimension_numbers=('NWC', 'WIO', 'NWC'), feature_group_count=D_CONV) + dw_b.astype(c.dtype)
    c = _layernorm(c, ln_g, ln_b)
    c = jax.nn.silu(c)
    return c @ w_conv_out

def _hybrid_mixer(h, w_in, a_re, a_im, log_dt, b_re, b_im, c_re, c_im, d_skip,
                  w_s5_lin, w_s5_gate, dw_w, dw_b, ln_g, ln_b, w_conv_out, w_out):
    z = h @ w_in
    s1 = D_SSM
    s2 = s1 + 2 * D_CONV
    s3 = s2 + D_MODEL
    u_s5, conv_in, gate_a, gate_b = z[..., :s1], z[..., s1:s2], z[..., s2:s3], z[..., s3:]
    ya = jax.nn.gelu(_s5_branch(u_s5, a_re, a_im, log_dt, b_re, b_im, c_re, c_im, d_skip), approximate=False)
    ya = (ya @ w_s5_lin) * jax.nn.sigmoid(ya @ w_s5_gate)
    yb = _conformer_branch(conv_in, dw_w, dw_b, ln_g, ln_b, w_conv_out)
    merged = jax.nn.sigmoid(gate_a) * ya + jax.nn.sigmoid(gate_b) * yb
    return merged @ w_out

def _moe(h, router_w, router_b, w_gate_up, b_gate_up, w_down, b_down):
    bsz, seq_len, d = h.shape
    hf = h.reshape(bsz * seq_len, d)
    logits = (hf @ router_w + router_b).astype(jnp.float32)
    top_val, top_idx = lax.top_k(logits, TOP_K)
    probs = jax.nn.softmax(top_val, axis=-1)
    combine = jnp.sum(jax.nn.one_hot(top_idx, N_EXPERTS, dtype=jnp.float32) * probs[..., None], axis=1)
    combine = combine.astype(h.dtype)
    out = jnp.zeros_like(hf)
    for e in range(N_EXPERTS):
        gu = hf @ w_gate_up[e] + b_gate_up[e]
        g, lin = gu[:, :D_EXPERT], gu[:, D_EXPERT:]
        g = jnp.minimum(g, SWIGLU_LIMIT)
        lin = jnp.clip(lin, -SWIGLU_LIMIT, SWIGLU_LIMIT)
        act = g * jax.nn.sigmoid(SWIGLU_ALPHA * g) * (lin + 1.0)
        out = out + combine[:, e:e + 1] * (act @ w_down[e] + b_down[e])
    return out.reshape(bsz, seq_len, d)

def setup_inputs(seed: int = 0) -> dict:
    key = jax.random.key(seed)
    ks = jax.random.split(key, 32)
    f32 = jnp.float32
    nrm = lambda k, shape, scale: scale * jax.random.normal(k, shape, f32)
    G, P, H = N_SSM_GROUPS, SSM_STATE, SSM_GROUP
    a_im = jnp.broadcast_to(math.pi * jnp.arange(P, dtype=f32), (DEPTH, G, P))
    return {
        "x": jax.random.normal(ks[0], (BATCH, SEQ, D_MODEL), f32),
        "meta_tokens": nrm(ks[1], (N_META, D_MODEL), 1.0),
        "norm_mix_g": 1.0 + nrm(ks[2], (DEPTH, D_MODEL), 0.02),
        "w_in": nrm(ks[3], (DEPTH, D_MODEL, D_IN_PROJ), D_MODEL ** -0.5),
        "ssm_a_re": -0.5 + nrm(ks[4], (DEPTH, G, P), 0.01),
        "ssm_a_im": a_im + nrm(ks[5], (DEPTH, G, P), 0.01),
        "ssm_log_dt": jax.random.uniform(ks[6], (DEPTH, G), f32, math.log(DT_MIN), math.log(DT_MAX)),
        "ssm_b_re": nrm(ks[7], (DEPTH, G, P, H), (2.0 * H) ** -0.5),
        "ssm_b_im": nrm(ks[8], (DEPTH, G, P, H), (2.0 * H) ** -0.5),
        "ssm_c_re": nrm(ks[9], (DEPTH, G, H, P), (2.0 * P) ** -0.5),
        "ssm_c_im": nrm(ks[10], (DEPTH, G, H, P), (2.0 * P) ** -0.5),
        "ssm_d": nrm(ks[11], (DEPTH, D_SSM), 1.0),
        "w_s5_lin": nrm(ks[12], (DEPTH, D_SSM, D_MODEL), D_SSM ** -0.5),
        "w_s5_gate": nrm(ks[13], (DEPTH, D_SSM, D_MODEL), D_SSM ** -0.5),
        "conv_dw_w": nrm(ks[14], (DEPTH, CONV_WIDTH, 1, D_CONV), CONV_WIDTH ** -0.5),
        "conv_dw_b": nrm(ks[15], (DEPTH, D_CONV), 0.02),
        "conv_ln_g": 1.0 + nrm(ks[16], (DEPTH, D_CONV), 0.02),
        "conv_ln_b": nrm(ks[17], (DEPTH, D_CONV), 0.02),
        "w_conv_out": nrm(ks[18], (DEPTH, D_CONV, D_MODEL), D_CONV ** -0.5),
        "w_out": nrm(ks[19], (DEPTH, D_MODEL, D_MODEL), D_MODEL ** -0.5),
        "norm_ffn_g": 1.0 + nrm(ks[20], (DEPTH, D_MODEL), 0.02),
        "router_w": nrm(ks[21], (DEPTH, D_MODEL, N_EXPERTS), D_MODEL ** -0.5),
        "router_b": nrm(ks[22], (DEPTH, N_EXPERTS), 0.01),
        "w_gate_up": nrm(ks[23], (DEPTH, N_EXPERTS, D_MODEL, 2 * D_EXPERT), D_MODEL ** -0.5),
        "b_gate_up": nrm(ks[24], (DEPTH, N_EXPERTS, 2 * D_EXPERT), 0.02),
        "w_down": nrm(ks[25], (DEPTH, N_EXPERTS, D_EXPERT, D_MODEL), D_EXPERT ** -0.5),
        "b_down": nrm(ks[26], (DEPTH, N_EXPERTS, D_MODEL), 0.02),
        "norm_final_g": 1.0 + nrm(ks[27], (D_MODEL,), 0.02),
    }

def reference(x, meta_tokens, norm_mix_g, w_in, ssm_a_re, ssm_a_im, ssm_log_dt, ssm_b_re, ssm_b_im,
              ssm_c_re, ssm_c_im, ssm_d, w_s5_lin, w_s5_gate, conv_dw_w, conv_dw_b, conv_ln_g, conv_ln_b,
              w_conv_out, w_out, norm_ffn_g, router_w, router_b, w_gate_up, b_gate_up, w_down, b_down,
              norm_final_g):
    bsz = x.shape[0]
    meta = jnp.broadcast_to(meta_tokens[None].astype(x.dtype), (bsz, N_META, D_MODEL))
    h = jnp.concatenate([meta, x], axis=1)
    for i in range(DEPTH):
        h = h + _hybrid_mixer(_rmsnorm(h, norm_mix_g[i]), w_in[i], ssm_a_re[i], ssm_a_im[i], ssm_log_dt[i],
                              ssm_b_re[i], ssm_b_im[i], ssm_c_re[i], ssm_c_im[i], ssm_d[i],
                              w_s5_lin[i], w_s5_gate[i], conv_dw_w[i], conv_dw_b[i], conv_ln_g[i], conv_ln_b[i],
                              w_conv_out[i], w_out[i])
        h = h + _moe(_rmsnorm(h, norm_ffn_g[i]), router_w[i], router_b[i], w_gate_up[i], b_gate_up[i],
                     w_down[i], b_down[i])
    return _rmsnorm(h, norm_final_g)[:, N_META:]


_drawn_inputs = setup_inputs


def setup_inputs(seed=0):
    import zlib

    import numpy as np

    out = dict(_drawn_inputs(seed))
    spreads = {}
    factors = {'ssm_a_re': 200.0,
     'conv_ln_g': 2.796,
     'conv_ln_b': 2.812,
     'b_gate_up': 5.378,
     'b_down': 6.191,
     'norm_final_g': 30.673,
     'ssm_a_im': 64.0,
     'ssm_log_dt': 34.8,
     'ssm_b_re': 47.648,
     'ssm_b_im': 48.56,
     'ssm_c_re': 52.68,
     'ssm_c_im': 64.0,
     'router_b': 3.254}
    for name, (base, spread) in spreads.items():
        noise = np.random.default_rng([zlib.crc32(name.encode()), seed]).standard_normal(out[name].shape)
        drawn = base * np.exp(spread * noise) if base else spread * noise
        out[name] = __import__('jax').numpy.asarray(drawn.astype(out[name].dtype))
    for name, factor in factors.items():
        out[name] = (out[name] * factor).astype(out[name].dtype)
    return out
```

```python
from contextlib import ExitStack

import numpy as np

import concourse.bass as bass
from concourse import mybir

F32 = mybir.dt.float32
BF16 = mybir.dt.bfloat16
I32 = mybir.dt.int32
ALU = mybir.AluOpType
ACT = mybir.ActivationFunctionType
AX_X = mybir.AxisListType.X

P = 128
D = 1024
KT = D // P
S = 256
ST = S // P
META = 16
L = S + META
DS = D // 2
MT = DS // P
NB = 16
QB = NB // MT
TAPS = 31
HALO = TAPS - 1 - META
EXP = 32
TOPK = 4
BS = 64
NBLK = EXP + (S * TOPK) // BS - 1
NBC = NBLK + 1
EPS_RMS, EPS_LN = 1e-6, 1e-5
LIMIT, ALPHA = 7.0, 1.702
SLOT = 2048
NSLOT = 12
MSLOT = 9
PE_TILES = 2
MAGIC = 1.5 * 2.0 ** 23
TWO_PI = (6.28125, 0.0019350051879882812, 3.0199159819567e-07)
LN2 = (0.693359375, -2.12194440e-4)
BIG = 9999.0


def build(nc, T, out):
    with ExitStack() as ctx:
        def sb(name, shape, dt=F32):
            return ctx.enter_context(nc.sbuf_tensor(name, shape, dt))

        def sem(name):
            return ctx.enter_context(nc.semaphore(name))

        ring = sb("ring", [P, NSLOT * SLOT])
        rA = sb("rA", [P, 4096])
        rB = sb("rB", [P, KT * L])
        rC = sb("rC", [P, 4096])
        rD = sb("rD", [P, 3 * QB * L])
        rE = sb("rE", [P, 2 * QB * L])
        rF = sb("rF", [P, 2 * QB * L])
        rG = sb("rG", [P, QB * L])
        rX = sb("rX", [P, 2048])
        rU = sb("rU", [P, MT * L])
        rP = sb("rP", [P, MT * (HALO + L)])
        rQ = sb("rQ", [P, MT * L])
        rY = sb("rY", [P, MT * S])
        rW = sb("rW", [P, 1024])

        def view(r, at, *dims, rows=P, dt=F32):
            n = 1
            for d in dims:
                n *= d
            words = n // 2 if dt == BF16 else n
            v = r[0:rows, at:at + words]
            if dt != F32:
                v = v.bitcast(dt)
            if len(dims) == 2:
                v = v.rearrange("p (a b) -> p a b", b=dims[1])
            if len(dims) == 3:
                v = v.rearrange("p (a b c) -> p a b c", b=dims[1], c=dims[2])
            if len(dims) == 4:
                v = v.rearrange("p (a b c d) -> p a b c d", b=dims[1], c=dims[2], d=dims[3])
            return v

        xin = view(rA, 0, 3, D)
        junk = view(rA, 3072, D)
        hT = view(rB, 0, KT, L)
        gates = view(rC, 0, 2 * KT, S)
        work = MSLOT * SLOT
        cosT = [view(rD, 0, QB, L), view(ring, work, QB, L)]
        sinT = [view(rD, QB * L, QB, L), view(ring, work + QB * L, QB, L)]
        taps = view(ring, work + 2 * QB * L, TAPS, P)
        tabtmp = view(rD, 2 * QB * L, QB, L)
        phase = view(rD, 2 * QB * L, NB, 33)
        drive = view(rE, 0, 2, QB, L)
        rot = view(rF, 0, 2, QB, L)
        rtmp = view(rG, 0, QB, L)
        prod = view(rA, 0, 2, 2, QB, S)
        uT = view(rU, 0, MT, L)
        cin = view(rP, 0, MT, HALO + L)
        cgate = view(rQ, 0, MT, L)
        cacc = view(rQ, 0, MT, S)
        ya = view(rY, 0, MT, S)
        merged = view(rB, 0, KT, S)
        csq = view(rE, 0, MT, S)
        lnr = view(rE, 1024, S)
        lnt = view(rE, 1280, S)
        lnv = view(rE, 1536, S)
        sig = view(rG, 0, 2, S)
        mtmp = view(rG, 512, 2, S)
        bq = view(rE, 0, 2, NB, 2, 16)
        cq = view(rE, 1024, 2, MT, 2, 64)
        bn = view(rF, 0, 2, NB, 16)
        cn = view(rF, 512, 2, MT, 64)
        pt1 = view(rF, 1024, NB, 16)
        pt2 = view(rF, 1280, NB, 16)
        bT = view(rX, 0, 2, MT, P)
        bz = view(rX, 1024, 2, QB, P)
        cT = view(rW, 0, 2, MT, P)
        h2 = view(rX, 0, ST, D)
        gffn = view(rF, 0, D)
        gfin = view(rF, D, D)
        bdown = view(rG, 0, D, rows=EXP)
        rw = view(rU, 0, KT, EXP)
        rb = view(rU, 256, EXP)
        bgu = view(rA, 0, 2 * D, rows=96)
        bg2 = view(rA, 2048, 2 * D, rows=96, dt=BF16)
        bp = view(rW, 0, 2 * D, rows=96, dt=BF16)
        hf = view(rA, 0, ST, D)
        hr = view(rA, 2048, ST, D)
        hfT = view(rB, 0, KT, S)
        hp = view(rC, 0, 3, ST, D, dt=BF16)
        g1 = view(rD, 0, 512)
        l1 = view(rD, 512, 512)
        sg = view(rD, 1024, 512)
        actT = view(rD, 1536, 4, P)
        ysb = view(rD, 2048, 512)
        xT = view(rD, 2560, KT, BS)
        upper = view(rP, 0, P, dt=BF16)
        onesb = view(rP, 64, P, dt=BF16)
        slots = view(rP, 128, 2, BS)
        blks = view(rP, 256, NBC)
        tri = view(rP, 304, EXP, rows=EXP)
        onehot = view(rE, 0, ST, BS, dt=BF16)
        wsel = view(rE, 64, ST, P)
        selT = view(rE, 320, 2, S)
        ebias = view(rE, 832, 2, P, dt=BF16)
        blkcol = view(rE, 960, 4, NBC)
        bk = view(rE, 1152, NBC)
        lg = view(rE, 1200, ST, EXP)
        gt = view(rE, 1264, ST, EXP)
        eq = view(rE, 1328, ST, EXP)
        ce = view(rE, 1392, ST, EXP)
        mask = view(rE, 1456, ST, EXP)
        ex = view(rE, 1520, ST, EXP)
        comb = view(rE, 1584, ST, EXP)
        posm = view(rE, 1648, ST, EXP)
        maskb = view(rE, 1712, ST, EXP, dt=BF16)
        cmp = view(rE, 1744, NBC, rows=EXP)
        off = view(rE, 1792, NBC)
        v8 = view(rE, 1840, ST, 8)
        rs1 = view(rE, 1856, 16)
        cur = view(rE, 1872, 4)
        cur2 = view(rE, 1876, 2)
        pcT = view(rQ, 0, 4, P, rows=EXP)
        nbb = view(rQ, 512, P, rows=EXP)
        ident = sb("ident", [P, P])
        ones = sb("ones", [P, P])
        invc = sb("invc", [P, P])
        seg = sb("seg", [P, 8])
        pidx = sb("pidx", [P, 1])
        expo = sb("expo", [P, 17])
        hmask = sb("hmask", [P, 2])
        jmask = sb("jmask", [P, 4])
        pmod = sb("pmod", [P, 1])
        es = sb("es", [P, NB, 33])
        ec = sb("ec", [P, NB, 33])
        colp = sb("colp", [P, 24])
        cw = sb("cw", [P, TAPS * MT])
        rows1 = view(rG, 0, P, rows=24)
        rows2 = view(rG, 128, P, rows=TAPS * MT)
        arow = view(rG, 256, 4, P, rows=NB)
        ldt = view(rG, 768, 2, rows=NB)
        dts = view(rG, 770, 2, rows=NB)
        xs = view(rG, 780, 6, 16)
        pc = sb("pc", [P, 4, NB])
        sp_ = sb("sp_", [P, 6, NB])
        xi = sb("xi", [P, NB], I32)
        ss = sb("ss", [P, 16])
        blk_expert = sb("blk_expert", [1, NBC], I32)
        blk_until = sb("blk_until", [1, EXP], I32)
        blk_last = sb("blk_last", [1, EXP], I32)
        decay, abr, abi, den, cre, cim = (sp_[:, n, :] for n in range(6))

        ps = ctx.enter_context(nc.psum_tensor("ps", [P, 8, 512], F32))

        x_in, par_in, xres_in, late_in = sem("x_in"), sem("par_in"), sem("xres_in"), sem("late_in")
        slot_in = [sem(f"slot_in{n}") for n in range(MSLOT)]
        gu_in = [sem(f"gu_in{n}") for n in range(KT)]
        dn_in = [sem(f"dn_in{n}") for n in range(KT)]
        pool_step, consts, tables, late_consts = sem("pool_step"), sem("consts"), sem("tables"), sem("late_consts")
        dve_step, act_step = sem("dve_step"), sem("act_step")
        sumsq, ms_ready, root, normed = sem("sumsq"), sem("ms_ready"), sem("root"), sem("normed")
        h_tr, h_act, h_dve = sem("h_tr"), sem("h_act"), sem("h_dve")
        par_tr, par_cols, disc_rows = sem("par_tr"), sem("par_cols"), sem("disc_rows")
        disc_tr, phases, sines, etab = sem("disc_tr"), sem("phases"), sem("sines"), sem("etab")
        bc_ready, bc_tr, bc_cols = sem("bc_ready"), sem("bc_tr"), sem("bc_cols")
        bz_ready, drive_mm, drive_sb, drive_used = sem("bz_ready"), sem("drive_mm"), sem("drive_sb"), sem("drive_used")
        tab_used, states, y_mm, y_pre, ya_ready = (sem("tab_used"), sem("states"), sem("y_mm"), sem("y_pre"),
                                                   sem("ya_ready"))
        mm, mm_act, mm_dve, wo_used = sem("mm"), sem("mm_act"), sem("mm_dve"), sem("wo_used")
        glu, conv_done, mean_mm, centred, squared, var_mm = (sem("glu"), sem("conv_done"), sem("mean_mm"),
                                                                   sem("centred"), sem("squared"), sem("var_mm"))
        var_ready, ln_root, ln_ready, conv_act = sem("var_ready"), sem("ln_root"), sem("ln_ready"), sem("conv_act")
        merge_ready, h2_ready, hf_ready, hf_tr = sem("merge_ready"), sem("h2_ready"), sem("hf_ready"), sem("hf_tr")
        hfT_act, hfT_dve, part1, rest1, part2, parts = (sem("hfT_act"), sem("hfT_dve"), sem("part1"), sem("rest1"),
                                                        sem("part2"), sem("parts"))
        logit_mm, top1, exps, masks, count_mm, pos_ready = (sem("logit_mm"), sem("top1"), sem("exps"), sem("masks"),
                                                            sem("count_mm"), sem("pos_ready"))
        plan_tr, plan_cols, plan_mm, plan_rows, plan_sel, plan = (sem("plan_tr"), sem("plan_cols"), sem("plan_mm"),
                                                                  sem("plan_rows"), sem("plan_sel"), sem("plan"))
        onehot_ready, gather_mm, xT_ready = sem("onehot_ready"), sem("gather_mm"), sem("xT_ready")
        gu_done, dn_done, g1_ready, sg_ready, act_ready = (sem("gu_done"), sem("dn_done"), sem("g1_ready"),
                                                           sem("sg_ready"), sem("act_ready"))
        wsel_ready, act_tr, sel_tr, actT_ready, selT_ready = (sem("wsel_ready"), sem("act_tr"), sem("sel_tr"),
                                                              sem("actT_ready"), sem("selT_ready"))
        y_ready, scattered, blk_step, l1_ready, m_ready = (sem("y_ready"), sem("scattered"), sem("blk_step"),
                                                           sem("l1_ready"), sem("m_ready"))
        stored = sem("stored")
        bq_zero, taps_ready, conv_mm, conv_sb = sem("bq_zero"), sem("taps_ready"), sem("conv_mm"), sem("conv_sb")

        w_in = T["w_in"][0].rearrange("(k p) n -> p k n", p=P)
        s5l = T["w_s5_lin"][0].rearrange("(k p) n -> p k n", p=P)
        s5g = T["w_s5_gate"][0].rearrange("(k p) n -> p k n", p=P)
        wco = T["w_conv_out"][0].rearrange("(k p) n -> p k n", p=P)
        wout = T["w_out"][0].rearrange("(k p) n -> p k n", p=P)
        in_cols = [0, 256, 512, 1024, 768, 1280] + [DS + 2 * DS + 256 * n for n in range(8)]
        loads = [w_in[:, :, c:c + 256] for c in in_cols]
        loads += [s5l[:, :, 0:512], s5g[:, :, 0:512], s5l[:, :, 512:1024], s5g[:, :, 512:1024]]
        loads += [wco[:, :, 0:512], wco[:, :, 512:1024]]
        loads += [wout[:, 2 * n:2 * n + 2, :] for n in range(4)]
        N_IN, N_LOADS = len(in_cols), len(loads)

        def slot(n, dims):
            return view(ring, (n % MSLOT) * SLOT, *dims)

        USES = ["act"] * (2 * N_IN) + ["dve", "act"] * KT + ["dve"] * KT + ["dve"] * 4
        S5_USE, CO_USE, WO_USE = 2 * N_IN, 2 * N_IN + 2 * KT, 2 * N_IN + 3 * KT

        def emptied(eng, use):
            who = USES[use]
            eng.wait_ge(mm_act if who == "act" else mm_dve, USES[:use + 1].count(who))

        def used_up(eng, n):
            if n < N_IN:
                eng.wait_ge(mm, 2 * n + 2)
            elif n < N_IN + 4:
                eng.wait_ge(mm, S5_USE + 8 * ((n - N_IN) // 2 + 1))
            elif n < N_IN + 6:
                eng.wait_ge(mm, CO_USE + 4 * (n - N_IN - 3))
            elif n < N_LOADS - 1:
                eng.wait_ge(wo_used, n - N_IN - 5)
            else:
                eng.wait_ge(mm, WO_USE + 4)

        gsl = [view(ring, k * SLOT, 4, 512) for k in range(KT)]
        dsl = [view(ring, KT * SLOT + k * 1024, 2, 512) for k in range(KT)]

        block = ctx.enter_context(nc.Block())

        @block.sync
        def _(sp):
            sp.dma_start(xin[0:P, 0, :], T["x"][0, 0:P, :]).then_inc(x_in, 16)
            sp.dma_start(xin[0:P, 1, :], T["x"][0, P:S, :]).then_inc(x_in, 16)
            sp.wait_ge(par_in, 16 * 13)

            def load(n):
                if n >= MSLOT:
                    used_up(sp, n - MSLOT)
                dims = (KT, 256) if n < N_IN else ((MT, 512) if n < N_LOADS - 4 else (2, 1024))
                sp.dma_start(slot(n, dims), loads[n]).then_inc(slot_in[n % MSLOT], 16)

            def first_gu(k):
                sp.dma_start(gsl[k], T["w_gate_up"][0, 0, k * P:(k + 1) * P, :].rearrange("p (a b) -> p a b", b=512)
                             ).then_inc(gu_in[k], 16)

            def first_dn(k):
                sp.dma_start(dsl[k], T["w_down"][0, 0, k * P:(k + 1) * P, :].rearrange("p (a b) -> p a b", b=512)
                             ).then_inc(dn_in[k], 16)

            for n in range(N_IN + 6):
                load(n)
            sp.wait_ge(drive_mm, 8 * MT)
            sp.dma_start(h2[:, 0, :], T["x"][0, 0:P, :]).then_inc(xres_in, 16)
            sp.dma_start(h2[:, 1, :], T["x"][0, P:S, :]).then_inc(xres_in, 16)
            sp.wait_ge(states, MT)
            sp.wait_ge(y_pre, MT)
            sp.wait_ge(y_mm, MT)
            sp.dma_start(gffn, T["norm_ffn_g"][0:1, :].to_broadcast([P, D])).then_inc(late_in, 16)
            sp.dma_start(gfin, T["norm_final_g"].rearrange("(a n) -> a n", a=1).to_broadcast([P, D])
                         ).then_inc(late_in, 16)
            sp.dma_start(rw, T["router_w"][0].rearrange("(k p) e -> p k e", p=P)).then_inc(late_in, 16)
            sp.dma_start(rb, T["router_b"][0:1, :].to_broadcast([P, EXP])).then_inc(late_in, 16)
            for c in range(3):
                sp.dma_start(bgu[32 * c:32 * c + 32, :], T["b_gate_up"][0]).then_inc(late_in, 16)
            sp.wait_ge(conv_mm, PE_TILES)
            for k in range(2, KT):
                first_dn(k)
            for n in range(N_IN + 6, N_LOADS):
                load(n)
            for k in (6, 7):
                used_up(sp, MSLOT + k)
                first_gu(k)
            used_up(sp, 2 * MSLOT - 1)
            for k in range(2):
                first_dn(k)
            for k in range(6):
                used_up(sp, 2 * MSLOT + k)
                first_gu(k)
            sp.wait_ge(merge_ready, KT + 1)
            sp.dma_start(bdown, T["b_down"][0]).then_inc(late_in, 16)
            sp.wait_ge(plan, 1)
            with sp.Fori(1, EXP) as e:
                last = sp.value_load(blk_last[0:1, bass.ds(e - 1, 1)], min_val=0, max_val=NBLK - 1)
                for k in range(KT):
                    sp.wait_ge(gu_done, last * KT + (k + 1))
                    sp.dma_start(gsl[k], T["w_gate_up"][0, bass.ds(e, 1), k * P:(k + 1) * P, :].rearrange(
                        "o p (a b) -> p (o a) b", b=512)).then_inc(gu_in[k], 16)
                for k in range(KT):
                    sp.wait_ge(dn_done, last * KT + (k + 1))
                    sp.dma_start(dsl[k], T["w_down"][0, bass.ds(e, 1), k * P:(k + 1) * P, :].rearrange(
                        "o p (a b) -> p (o a) b", b=512)).then_inc(dn_in[k], 16)
            for c in range(ST):
                sp.wait_ge(h2_ready, 5 + c)
                sp.dma_start(out[0, c * P:(c + 1) * P, :], h2[:, c, :]).then_inc(stored, 16)
            sp.wait_ge(stored, 16 * ST)

        @block.gpsimd
        def _(pool):
            n = [0]

            def link(ins):
                n[0] += 1
                ins.then_inc(pool_step, 1)
                pool.wait_ge(pool_step, n[0])

            link(nc.gpsimd.memset(ident[:, :], 0.0))
            nc.gpsimd.affine_select(out=ident[:, :], in_=ident[:, :], compare_op=ALU.not_equal, fill=1.0, base=0,
                                    pattern=[[-1, P]], channel_multiplier=1).then_inc(consts, 1)
            nc.gpsimd.memset(ones[:, :], 1.0).then_inc(consts, 1)
            nc.gpsimd.memset(invc[:, :], 1.0 / DS).then_inc(consts, 1)
            nc.gpsimd.iota(pidx[:, :], pattern=[[0, 1]], base=0, channel_multiplier=1,
                           allow_small_or_imprecise_dtypes=True).then_inc(consts, 1)
            nc.gpsimd.iota(expo[:, :], pattern=[[1, 17]], base=0, channel_multiplier=0,
                           allow_small_or_imprecise_dtypes=True).then_inc(consts, 1)
            link(nc.gpsimd.memset(seg[:, :], 1.0))
            link(nc.gpsimd.affine_select(out=seg[:, :], in_=seg[:, :], compare_op=ALU.is_ge, fill=0.0, base=0,
                                         pattern=[[-16, 8]], channel_multiplier=1))
            nc.gpsimd.affine_select(out=seg[:, :], in_=seg[:, :], compare_op=ALU.is_ge, fill=0.0, base=15,
                                    pattern=[[16, 8]], channel_multiplier=-1).then_inc(consts, 1)
            nc.gpsimd.memset(cin[:, :, 0:HALO], 0.0).then_inc(consts, 1)
            nc.gpsimd.memset(bq, 0.0).then_inc(bq_zero, 1)
            pool.wait_ge(etab, 1)

            def table(q):
                if q >= 2:
                    pool.wait_ge(tab_used, q - 1)
                ct, st = cosT[q % 2], sinT[q % 2]

                def e1(t):
                    return t[:, q * QB:(q + 1) * QB, 0:17].unsqueeze(3).to_broadcast([P, QB, 17, 16])

                def e2(t):
                    return t[:, q * QB:(q + 1) * QB, 17:33].unsqueeze(2).to_broadcast([P, QB, 17, 16])

                def grid(t):
                    return t.rearrange("p j (a b) -> p j a b", b=16)

                nc.gpsimd.tensor_tensor(grid(ct), e1(ec), e2(ec), ALU.mult)
                link(nc.gpsimd.tensor_tensor(grid(tabtmp), e1(es), e2(es), ALU.mult))
                link(nc.gpsimd.tensor_tensor(grid(ct), grid(ct), grid(tabtmp), ALU.subtract))
                nc.gpsimd.tensor_tensor(grid(st), e1(es), e2(ec), ALU.mult)
                link(nc.gpsimd.tensor_tensor(grid(tabtmp), e1(ec), e2(es), ALU.mult))
                link(nc.gpsimd.tensor_tensor(grid(st), grid(st), grid(tabtmp), ALU.add))
                nc.gpsimd.engine_nop().then_inc(tables, 1)

            def tap_matrices(m):
                nc.gpsimd.tensor_tensor(taps, ident[:, :].unsqueeze(1).to_broadcast([P, TAPS, P]),
                                        cw[:, m::MT].unsqueeze(2).to_broadcast([P, TAPS, P]), ALU.mult
                                        ).then_inc(taps_ready, 1)

            table(0)
            table(1)
            pool.wait_ge(par_cols, 2)
            tap_matrices(MT - 1)
            pool.wait_ge(mm_act, 12)
            nc.gpsimd.tensor_tensor(cin[:, :, HALO:], cin[:, :, HALO:], cgate, ALU.mult).then_inc(glu, 1)
            table(2)
            pool.wait_ge(conv_mm, 1)
            tap_matrices(MT - 2)
            table(3)
            pool.wait_ge(conv_done, 1)
            pool.wait_ge(conv_mm, PE_TILES)
            link(nc.gpsimd.memset(upper, 1.0))
            nc.gpsimd.affine_select(out=upper, in_=upper, compare_op=ALU.is_gt, fill=0.0, base=0,
                                    pattern=[[1, P]], channel_multiplier=-1).then_inc(late_consts, 1)
            nc.gpsimd.memset(onesb, 1.0).then_inc(late_consts, 1)
            nc.gpsimd.iota(slots, pattern=[[0, 2], [1, BS]], base=0, channel_multiplier=0,
                           allow_small_or_imprecise_dtypes=True).then_inc(late_consts, 1)
            nc.gpsimd.iota(blks, pattern=[[1, NBC]], base=0, channel_multiplier=0,
                           allow_small_or_imprecise_dtypes=True).then_inc(late_consts, 1)
            link(nc.gpsimd.memset(tri, 1.0))
            nc.gpsimd.affine_select(out=tri, in_=tri, compare_op=ALU.is_ge, fill=0.0, base=0,
                                    pattern=[[1, EXP]], channel_multiplier=-1).then_inc(late_consts, 1)
            pool.wait_ge(ln_ready, 1)
            nc.gpsimd.memset(ebias, 0.0).then_inc(late_consts, 1)
            nc.gpsimd.memset(selT, 0.0).then_inc(selT_ready, 1)
            nc.gpsimd.memset(ysb, 0.0).then_inc(y_ready, 1)
            pool.wait_ge(part1, 1)
            nc.gpsimd.tensor_tensor(hr, hf, hp[:, 0, :, :], ALU.subtract).then_inc(rest1, 1)
            pool.wait_ge(part2, 1)
            nc.gpsimd.tensor_tensor(hp[:, 2, :, :], hr, hp[:, 1, :, :], ALU.subtract).then_inc(parts, 1)

        @block.scalar
        def _(act):
            act.dma_start(xin[0:META, 2, :], T["meta_tokens"]).then_inc(x_in, 16)
            r1 = (("norm_mix_g", 0, 8), ("ssm_d", 8, 4), ("conv_dw_b", 12, 4), ("conv_ln_g", 16, 4),
                  ("conv_ln_b", 20, 4))
            act.dma_start(ldt, T["ssm_log_dt"].rearrange("o (b g) -> (o b) g", g=2)).then_inc(par_in, 16)
            act.dma_start(arow[:, 2, :], T["ssm_a_re"].rearrange("o (b g) p -> (o b) (g p)", g=2)).then_inc(par_in, 16)
            act.dma_start(arow[:, 3, :], T["ssm_a_im"].rearrange("o (b g) p -> (o b) (g p)", g=2)).then_inc(par_in, 16)
            for name, at, n in r1:
                act.dma_start(rows1[at:at + n, :], T[name].rearrange("o (m p) -> (o m) p", p=P)).then_inc(par_in, 16)
            act.dma_start(rows2, T["conv_dw_w"].rearrange("o j u (m p) -> (o j u m) p", p=P)).then_inc(par_in, 16)
            for n, (b, c) in enumerate((("ssm_b_re", "ssm_c_re"), ("ssm_b_im", "ssm_c_im"))):
                act.dma_start(bn[:, n, :, :], T[b][0].rearrange("g p h -> (g p) h").rearrange("(b q) h -> q b h", q=P)
                              ).then_inc(par_in, 16)
                act.dma_start(cn[:, n, :, :], T[c][0].rearrange("g h p -> (g h) p").rearrange("(m q) p -> q m p", q=P)
                              ).then_inc(par_in, 16)
            n = [0]

            def link(ins):
                n[0] += 1
                ins.then_inc(act_step, 1)
                act.wait_ge(act_step, n[0])

            act.wait_ge(x_in, 48)
            act.wait_ge(dve_step, 1)
            for c in range(3):
                rows = P if c < 2 else META
                link(nc.scalar.activation(junk[0:rows, :], xin[0:rows, c, :], ACT.Square,
                                          accum_out=ss[0:rows, c:c + 1]))
            nc.scalar.copy(ss[:, 3:6], ss[:, 0:3]).then_inc(sumsq, 1)
            act.wait_ge(ms_ready, 1)
            nc.scalar.activation(ss[:, 9:12], ss[:, 6:9], ACT.Sqrt).then_inc(root, 1)
            act.wait_ge(par_cols, 1)
            for k in range(1, KT, 2):
                act.wait_ge(h_tr, k + 1)
                nc.scalar.activation(hT[:, k, :], ps[:, k % 4, 0:L], ACT.Copy, scale=colp[:, k:k + 1]).then_inc(h_act, 1)
            act.wait_ge(phases, 1)
            nc.scalar.activation(es[:, :, :], phase, ACT.Sin).then_inc(sines, 1)
            nc.scalar.activation(ec[:, :, :], phase, ACT.Sin, scale=0.5).then_inc(sines, 1)

            def empty_z(z):
                act.wait_ge(mm, z + 1)
                b = z % 4
                if z < 4:
                    ins = nc.scalar.copy(uT[:, z, :], ps[:, b, 0:L])
                elif z < 12:
                    m = 2 * ((z - 4) // 4) + z % 2
                    if (z - 4) % 4 < 2:
                        ins = nc.scalar.copy(cin[:, m, HALO:], ps[:, b, 0:L])
                    else:
                        ins = nc.scalar.activation(cgate[:, m, :], ps[:, b, 0:L], ACT.Sigmoid)
                else:
                    ins = nc.scalar.activation(gates[:, z - 12, :], ps[:, b, 0:S], ACT.Sigmoid)
                ins.then_inc(mm_act, 1)

            def empty_drive(q):
                if q == 0:
                    act.wait_ge(bc_tr, 16)
                if q:
                    act.wait_ge(drive_used, q)
                for n in range(8):
                    act.wait_ge(drive_mm, 8 * q + n + 1)
                    nc.scalar.copy(drive[:, n % 2, n // 2, :], ps[:, 4 + n % 2, 0:L]).then_inc(drive_sb, 1)

            def gelu(q):
                act.wait_ge(y_pre, q + 1)
                nc.scalar.activation(ya[:, q, :], ya[:, q, :], ACT.Gelu).then_inc(ya_ready, 1)

            def empty_conv(n):
                m = MT - 1 - n
                act.wait_ge(conv_mm, n + 1)
                act.wait_ge(glu, 1)
                nc.scalar.activation(cacc[:, m, :], ps[:, 7, 0:S], ACT.Identity, bias=colp[:, 12 + m:13 + m]
                                     ).then_inc(conv_sb, 1)

            for z in range(8):
                empty_z(z)
            act.wait_ge(bc_tr, 16)
            nc.scalar.copy(bT[:, :, :, :], ps[:, 4:6, :].rearrange("p a (m c) -> p a m c", c=P)).then_inc(bc_cols, 1)
            nc.scalar.copy(cT[:, :, :, :], ps[:, 6:8, :].rearrange("p a (m c) -> p a m c", c=P)).then_inc(bc_cols, 1)
            empty_drive(0)
            for z in range(8, 12):
                empty_z(z)
            empty_drive(1)
            for z in range(12, 16):
                empty_z(z)
            empty_drive(2)
            empty_conv(0)
            for z in range(16, 20):
                empty_z(z)
            empty_drive(3)
            empty_conv(1)
            for z in range(20, 2 * N_IN):
                empty_z(z)
            for q in range(MT):
                gelu(q)

            def s5_gate(k):
                act.wait_ge(mm, S5_USE + 2 * k + 2)
                if k >= 2:
                    act.wait_ge(merge_ready, k - 1)
                nc.scalar.activation(sig[:, k % 2, :], ps[:, (S5_USE + 2 * k + 1) % 4, 0:S], ACT.Sigmoid
                                     ).then_inc(mm_act, 1)

            for k in range(4):
                s5_gate(k)
            act.wait_ge(centred, 1)
            nc.scalar.activation(csq, cacc, ACT.Square).then_inc(squared, 1)
            act.wait_ge(var_ready, 1)
            nc.scalar.activation(lnr, lnv, ACT.Sqrt).then_inc(ln_root, 1)
            act.wait_ge(ln_ready, 1)
            for m in range(MT):
                nc.scalar.activation(cacc[:, m, :], cacc[:, m, :], ACT.Silu, scale=colp[:, 16 + m:17 + m],
                                     bias=colp[:, 20 + m:21 + m]).then_inc(conv_act, 1)
            for k in range(4, KT):
                s5_gate(k)
            for c in range(ST):
                act.wait_ge(h2_ready, c + 1)
                act.wait_ge(hf_ready, 1)
                nc.scalar.activation(hr[:, c, :], h2[:, c, :], ACT.Square, accum_out=ss[:, c:c + 1]).then_inc(sumsq, 1)
            act.wait_ge(ms_ready, 2)
            nc.scalar.activation(ss[:, 9:11], ss[:, 6:8], ACT.Sqrt).then_inc(root, 1)
            act.wait_ge(hf_ready, 3)
            for b in range(0, 4, 2):
                act.wait_ge(hf_tr, b + 1)
                nc.scalar.copy(hfT[:, 2 * b:2 * b + 2, :], ps[:, 4 + b, :].rearrange("p (k t) -> p k t", t=S)
                               ).then_inc(hfT_act, 1)
            nc.scalar.copy(hp[:, 0, :, :], hf).then_inc(part1, 1)
            act.wait_ge(top1, 1)
            for c in range(ST):
                nc.scalar.activation(ex[:, c, :], lg[:, c, :], ACT.Exp, bias=rs1[:, c:c + 1]).then_inc(exps, 1)
            act.wait_ge(rest1, 1)
            nc.scalar.copy(hp[:, 1, :, :], hr).then_inc(part2, 1)

            act.wait_ge(gather_mm, 1)
            nc.scalar.copy(xT, ps[:, 3, :].rearrange("p (k s) -> p k s", s=BS)).then_inc(xT_ready, 1)
            act.wait_ge(plan, 1)
            total = act.value_load(blk_until[0:1, EXP - 1:EXP], min_val=EXP, max_val=NBLK)
            with act.Fori(0, NBLK) as i:
                with act.If(i < total):
                    act.wait_ge(g1_ready, i + 1)
                    nc.scalar.activation(sg, g1, ACT.Sigmoid, scale=ALPHA).then_inc(sg_ready, 1)
                    act.wait_ge(gather_mm, i + 2)
                    nc.scalar.copy(xT, ps[:, 3, :].rearrange("p (k s) -> p k s", s=BS)).then_inc(xT_ready, 1)
                    act.wait_ge(act_tr, i + 1)
                    nc.scalar.copy(actT, ps[:, 0, :].rearrange("p (j s) -> p j s", s=P)).then_inc(actT_ready, 1)
                    act.wait_ge(dn_done, i * KT + KT)
                    nc.scalar.copy(ysb, ps[:, 2, :]).then_inc(y_ready, 1)
            for c in range(ST):
                act.wait_ge(h2_ready, 3 + c)
                nc.scalar.activation(hf[:, c, :], h2[:, c, :], ACT.Square, accum_out=ss[:, c:c + 1]).then_inc(sumsq, 1)
            act.wait_ge(ms_ready, 3)
            nc.scalar.activation(ss[:, 9:11], ss[:, 6:8], ACT.Sqrt).then_inc(root, 1)

        @block.vector
        def _(dve):
            n = [0]

            def link(ins):
                n[0] += 1
                ins.then_inc(dve_step, 1)
                dve.wait_ge(dve_step, n[0])

            def rsqrt(width):
                a, r, o, t = (ss[:, k:k + width] for k in (6, 9, 12, 9))
                link(nc.vector.reciprocal(o, r))
                link(nc.vector.tensor_tensor(t, a, o, ALU.mult))
                link(nc.vector.tensor_tensor(t, t, o, ALU.mult))
                link(nc.vector.tensor_scalar(t, t, -0.5, 1.5, ALU.mult, ALU.add))
                link(nc.vector.tensor_tensor(o, o, t, ALU.mult))

            def exp(o, x, w, rows):
                y, k, r, p = (xs[0:rows, c, 0:w] for c in range(4))
                ki = xi[0:rows, 0:w]
                link(nc.vector.tensor_scalar(y, x, -88.0, 88.0, ALU.max, ALU.min))
                link(nc.vector.tensor_scalar(k, y, 1.4426950408889634, MAGIC, ALU.mult, ALU.add))
                link(nc.vector.tensor_scalar(k, k, -MAGIC, None, ALU.add))
                link(nc.vector.scalar_tensor_tensor(r, k, -LN2[0], y, ALU.mult, ALU.add))
                link(nc.vector.scalar_tensor_tensor(r, k, -LN2[1], r, ALU.mult, ALU.add))
                fact = [1.0]
                for c in range(1, 9):
                    fact.append(fact[-1] / c)
                link(nc.vector.tensor_scalar(p, r, fact[8], None, ALU.mult))
                for c in range(7, 0, -1):
                    link(nc.vector.scalar_tensor_tensor(p, p, fact[c], r, ALU.add, ALU.mult))
                link(nc.vector.tensor_scalar(p, p, 1.0, None, ALU.add))
                link(nc.vector.tensor_scalar(ki, k, 127.0, None, ALU.add))
                link(nc.vector.tensor_scalar(ki, ki, 23, None, ALU.logical_shift_left))
                link(nc.vector.tensor_tensor(o, p, ki.bitcast(F32), ALU.mult))

            def wrap(x, k):
                link(nc.vector.tensor_scalar(k, x, 1.0 / (2 * np.pi), MAGIC, ALU.mult, ALU.add))
                link(nc.vector.tensor_scalar(k, k, -MAGIC, None, ALU.add))
                for c in TWO_PI:
                    link(nc.vector.scalar_tensor_tensor(x, k, -c, x, ALU.mult, ALU.add))
                link(nc.vector.tensor_scalar(x, x, -3.1415925, 3.1415925, ALU.max, ALU.min))

            link(nc.vector.memset(ss[:, :], 1.0))
            dve.wait_ge(par_in, 16 * 13)
            exp(dts, ldt, 2, NB)
            for c in range(2):
                ins = nc.vector.tensor_tensor(arow[:, c, :].rearrange("b (g p) -> b g p", g=2),
                                              arow[:, 2 + c, :].rearrange("b (g p) -> b g p", g=2),
                                              dts.unsqueeze(2).to_broadcast([NB, 2, 64]), ALU.mult)
            ins.then_inc(disc_rows, 1)
            dve.wait_ge(sumsq, 1)
            link(nc.vector.tensor_scalar(ss[:, 6:9], ss[:, 3:6], 1.0 / D, EPS_RMS, ALU.mult, ALU.add))
            nc.vector.engine_nop().then_inc(ms_ready, 1)
            dve.wait_ge(root, 1)
            rsqrt(3)
            for c in range(3):
                rows = P if c < 2 else META
                nc.vector.tensor_scalar(xin[0:rows, c, :], xin[0:rows, c, :], ss[0:rows, 12 + c:13 + c], None,
                                        ALU.mult).then_inc(normed, 1)
            dve.wait_ge(par_tr, 2)
            nc.vector.tensor_copy(colp[:, :], ps[:, 7, 0:24]).then_inc(par_cols, 1)
            dve.wait_ge(par_cols, 1)
            nc.vector.tensor_copy(cw[:, :], ps[:, 7, 32:32 + TAPS * MT]).then_inc(par_cols, 1)
            for k in range(0, KT, 2):
                dve.wait_ge(h_tr, k + 1)
                nc.vector.tensor_scalar(hT[:, k, :], ps[:, k % 4, 0:L], colp[:, k:k + 1], None, ALU.mult
                                        ).then_inc(h_dve, 1)
            dve.wait_ge(consts, 7)
            link(nc.vector.tensor_reduce(hmask[:, :], seg[:, :].rearrange("p (j h) -> p h j", h=2), AX_X, ALU.add))
            link(nc.vector.tensor_reduce(jmask[:, :], seg[:, :].rearrange("p (j h) -> p j h", h=2), AX_X, ALU.add))
            link(nc.vector.tensor_copy(pmod[:, :], pidx[:, :]))
            for j in range(1, 4):
                link(nc.vector.scalar_tensor_tensor(pmod[:, :], jmask[:, j:j + 1], -32.0 * j, pmod[:, :], ALU.mult,
                                                    ALU.add))
            dve.wait_ge(disc_tr, 1)
            link(nc.vector.tensor_copy(pc[:, :, :], ps[:, 6, 0:4 * NB].rearrange("p (a b) -> p a b", b=NB)))
            exp(decay, pc[:, 0, :], NB, P)
            th = pc[:, 1, :]
            t16, kk = xs[:, 4, :], xs[:, 5, :]
            wrap(th, kk)
            link(nc.vector.tensor_scalar(t16, th, 16.0, None, ALU.mult))
            wrap(t16, kk)
            link(nc.vector.tensor_tensor(phase[:, :, 0:17], t16.unsqueeze(2).to_broadcast([P, NB, 17]),
                                         expo[:, :].unsqueeze(1).to_broadcast([P, NB, 17]), ALU.mult))
            link(nc.vector.tensor_tensor(phase[:, :, 17:33], th.unsqueeze(2).to_broadcast([P, NB, 16]),
                                         expo[:, 0:16].unsqueeze(1).to_broadcast([P, NB, 16]), ALU.mult))
            wrap(phase, es[:, :, :])
            nc.vector.engine_nop().then_inc(phases, 1)
            dve.wait_ge(sines, 2)
            link(nc.vector.tensor_tensor(ec[:, :, :], ec[:, :, :], ec[:, :, :], ALU.mult))
            nc.vector.tensor_scalar(ec[:, :, :], ec[:, :, :], -2.0, 1.0, ALU.mult, ALU.add).then_inc(etab, 1)
            dve.wait_ge(etab, 1)
            are, aim = pc[:, 2, :], pc[:, 3, :]
            t0, t1 = xs[:, 0, :], xs[:, 1, :]
            TT = nc.vector.tensor_tensor
            link(TT(abr, decay, ec[:, :, 18], ALU.mult))
            link(TT(abi, decay, es[:, :, 18], ALU.mult))
            link(nc.vector.tensor_scalar(abr, abr, -1.0, None, ALU.add))
            link(TT(den, are, are, ALU.mult))
            link(TT(t0, aim, aim, ALU.mult))
            link(TT(den, den, t0, ALU.add))
            link(nc.vector.reciprocal(t0, den))
            link(TT(cre, abr, are, ALU.mult))
            link(TT(t1, abi, aim, ALU.mult))
            link(TT(cre, cre, t1, ALU.add))
            link(TT(cre, cre, t0, ALU.mult))
            link(TT(cim, abi, are, ALU.mult))
            link(TT(t1, abr, aim, ALU.mult))
            link(TT(cim, cim, t1, ALU.subtract))
            link(TT(cim, cim, t0, ALU.mult))
            dve.wait_ge(bq_zero, 1)
            crb = cre.unsqueeze(2).to_broadcast([P, NB, 16])
            cib = cim.unsqueeze(2).to_broadcast([P, NB, 16])
            for ri, op in ((0, ALU.subtract), (1, ALU.add)):
                link(TT(pt1, crb, bn[:, ri, :, :], ALU.mult))
                link(TT(pt2, cib, bn[:, 1 - ri, :, :], ALU.mult))
                for g in range(2):
                    link(TT(bq[64 * g:64 * g + 64, ri, :, g, :], pt1[64 * g:64 * g + 64], pt2[64 * g:64 * g + 64], op))
            for g in range(2):
                for ri, sign in ((0, 1.0), (1, -1.0)):
                    link(nc.vector.tensor_scalar(cq[:, ri, :, g, :], cn[:, ri, :, :], hmask[:, g:g + 1], sign,
                                                 ALU.mult, ALU.mult))
            nc.vector.engine_nop().then_inc(bc_ready, 1)

            dve.wait_ge(bc_cols, 2)

            def spread_b(q):
                if q:
                    dve.wait_ge(drive_mm, 8 * q)
                for ri in range(2):
                    ins = TT(bz[:, ri, :, :], bT[:, ri, q:q + 1, :].to_broadcast([P, QB, P]),
                             jmask[:, :].unsqueeze(2).to_broadcast([P, QB, P]), ALU.mult)
                ins.then_inc(bz_ready, 1)

            def ypre(q):
                dve.wait_ge(y_mm, q + 1)
                nc.vector.scalar_tensor_tensor(ya[:, q, :], uT[:, q, META:], colp[:, 8 + q:9 + q], ps[:, 6, 0:S],
                                               ALU.mult, ALU.add).then_inc(y_pre, 1)

            spread_b(0)
            for q in range(MT):
                dve.wait_ge(drive_sb, 8 * (q + 1))
                dve.wait_ge(tables, q + 1)
                ct, st = cosT[q % 2], sinT[q % 2]
                if q + 1 < MT:
                    spread_b(q + 1)
                TT(rot[:, 0, :, :], drive[:, 0, :, :], ct, ALU.mult)
                link(TT(rtmp, drive[:, 1, :, :], st, ALU.mult))
                link(TT(rot[:, 0, :, :], rot[:, 0, :, :], rtmp, ALU.add))
                TT(rot[:, 1, :, :], drive[:, 1, :, :], ct, ALU.mult)
                link(TT(rtmp, drive[:, 0, :, :], st, ALU.mult))
                nc.vector.engine_nop().then_inc(drive_used, 1)
                link(TT(rot[:, 1, :, :], rot[:, 1, :, :], rtmp, ALU.subtract))
                for j in range(QB):
                    for ri in range(2):
                        ins = nc.vector.tensor_tensor_scan(
                            rot[:, ri, j, :], decay[:, q * QB + j:q * QB + j + 1].to_broadcast([P, L]),
                            rot[:, ri, j, :], 0.0, ALU.mult, ALU.add)
                link(ins)
                wr, wi = rot[:, 0, :, META:], rot[:, 1, :, META:]
                cs, sn, tm = ct[:, :, META:], st[:, :, META:], rtmp[:, :, META:]
                pr, pi = prod[:, q % 2, 0, :, :], prod[:, q % 2, 1, :, :]
                if q == 0:
                    dve.wait_ge(h_tr, KT)
                else:
                    if q >= 2:
                        dve.wait_ge(y_mm, q - 1)
                TT(pr, wr, cs, ALU.mult)
                link(TT(tm, wi, sn, ALU.mult))
                link(TT(pr, pr, tm, ALU.subtract))
                TT(pi, wr, sn, ALU.mult)
                link(TT(tm, wi, cs, ALU.mult))
                link(TT(pi, pi, tm, ALU.add))
                nc.vector.engine_nop().then_inc(states, 1)
                nc.vector.engine_nop().then_inc(tab_used, 1)
                if q:
                    ypre(q - 1)
            ypre(MT - 1)

            dve.wait_ge(glu, 1)
            for j in range(TAPS):
                for m in range(MT - PE_TILES):
                    w = cw[:, j * MT + m:j * MT + m + 1]
                    src = cin[:, m, j:j + S]
                    if j == 0:
                        ins = nc.vector.tensor_scalar(cacc[:, m, :], src, w, colp[:, 12 + m:13 + m], ALU.mult, ALU.add)
                    else:
                        dve.wait_ge(dve_step, n[0] - (MT - PE_TILES) + 1)
                        ins = nc.vector.scalar_tensor_tensor(cacc[:, m, :], src, w, cacc[:, m, :], ALU.mult, ALU.add)
                    ins.then_inc(dve_step, 1)
                    n[0] += 1
            dve.wait_ge(dve_step, n[0])
            nc.vector.engine_nop().then_inc(conv_done, 1)

            def s5_merge(n):
                use = S5_USE + 2 * n
                dve.wait_ge(mm, use + 1)
                emptied(dve, use + 1)
                link(TT(mtmp[:, 0, :], ps[:, use % 4, 0:S], sig[:, n % 2, :], ALU.mult))
                nc.vector.engine_nop().then_inc(mm_dve, 1)
                TT(merged[:, n, :], mtmp[:, 0, :], gates[:, n, :], ALU.mult).then_inc(merge_ready, 1)
                dve.wait_ge(merge_ready, n + 1)

            for n_ in range(2):
                s5_merge(n_)
            dve.wait_ge(mean_mm, 1)
            nc.vector.tensor_tensor(cacc, cacc, ps[:, 7:8, 0:S].to_broadcast([P, MT, S]), ALU.subtract
                                    ).then_inc(centred, 1)
            for n_ in range(2, 4):
                s5_merge(n_)
            dve.wait_ge(var_mm, 1)
            nc.vector.tensor_scalar(lnv, ps[:, 7, S:2 * S], EPS_LN, None, ALU.add).then_inc(var_ready, 1)
            dve.wait_ge(ln_root, 1)
            link(nc.vector.reciprocal(lnt, lnr))
            link(TT(lnr, lnv, lnt, ALU.mult))
            link(TT(lnr, lnr, lnt, ALU.mult))
            link(nc.vector.tensor_scalar(lnr, lnr, -0.5, 1.5, ALU.mult, ALU.add))
            link(TT(lnt, lnt, lnr, ALU.mult))
            TT(cacc, cacc, lnt.unsqueeze(1).to_broadcast([P, MT, S]), ALU.mult).then_inc(ln_ready, 1)
            for n_ in range(4, KT):
                s5_merge(n_)
            for m in range(KT):
                use = CO_USE + m
                dve.wait_ge(mm, use + 1)
                link(TT(mtmp[:, 1, :], ps[:, use % 4, 0:S], gates[:, KT + m, :], ALU.mult))
                nc.vector.engine_nop().then_inc(mm_dve, 1)
                link(TT(merged[:, m, :], merged[:, m, :], mtmp[:, 1, :], ALU.add))
            nc.vector.engine_nop().then_inc(merge_ready, 1)

            dve.wait_ge(late_in, 16 * 7)
            dve.wait_ge(y_mm, MT)
            link(nc.vector.tensor_copy(bp, bgu))
            link(TT(bgu, bgu, bp, ALU.subtract))
            link(nc.vector.tensor_copy(bg2, bgu))
            link(TT(bgu, bgu, bg2, ALU.subtract))
            link(nc.vector.tensor_copy(bp[32:64, :], bg2[32:64, :]))
            link(nc.vector.tensor_copy(bp[64:96, :], bgu[64:96, :]))
            nc.vector.engine_nop().then_inc(hf_ready, 1)

            dve.wait_ge(xres_in, 32)
            for c in range(ST):
                for h in range(2):
                    use = WO_USE + 2 * c + h
                    dve.wait_ge(mm, use + 1)
                    part = h2[:, c, 512 * h:512 * h + 512]
                    link(TT(part, part, ps[:, use % 4, :], ALU.add))
                nc.vector.engine_nop().then_inc(h2_ready, 1)
            dve.wait_ge(sumsq, 3)
            nc.vector.tensor_scalar(ss[:, 6:8], ss[:, 0:2], 1.0 / D, EPS_RMS, ALU.mult, ALU.add).then_inc(ms_ready, 1)
            dve.wait_ge(root, 2)
            rsqrt(2)
            for c in range(ST):
                nc.vector.scalar_tensor_tensor(hf[:, c, :], h2[:, c, :], ss[:, 12 + c:13 + c], gffn, ALU.mult,
                                               ALU.mult).then_inc(hf_ready, 1)
            dve.wait_ge(hf_ready, 3)
            for b in range(1, 4, 2):
                dve.wait_ge(hf_tr, b + 1)
                nc.vector.tensor_copy(hfT[:, 2 * b:2 * b + 2, :], ps[:, 4 + b, :].rearrange("p (k t) -> p k t", t=S)
                                      ).then_inc(hfT_dve, 1)
            dve.wait_ge(late_consts, 6)
            dve.wait_ge(logit_mm, 1)
            link(TT(lg, ps[:, 0, 0:ST * EXP].rearrange("p (c e) -> p c e", e=EXP),
                    rb.unsqueeze(1).to_broadcast([P, ST, EXP]), ALU.add))
            for c in range(ST):
                ins = nc.vector.max(v8[:, c, :], lg[:, c, :])
            link(ins)
            nc.vector.tensor_scalar(rs1[:, 0:2], v8[:, :, 0], -1.0, None, ALU.mult).then_inc(top1, 1)
            v4 = v8[:, :, TOPK - 1:TOPK].to_broadcast([P, ST, EXP])
            TT(eq, lg, v4, ALU.is_equal)
            link(TT(gt, lg, v4, ALU.is_gt))
            nc.vector.tensor_reduce(rs1[:, 2:4], gt, AX_X, ALU.add)
            for c in range(ST):
                ins = nc.vector.tensor_tensor_scan(ce[:, c, :], ones[:, 0:EXP], eq[:, c, :], 0.0, ALU.mult, ALU.add)
            link(ins)
            link(nc.vector.tensor_scalar(rs1[:, 4:6], rs1[:, 2:4], -1.0, float(TOPK), ALU.mult, ALU.add))
            link(TT(ce, ce, rs1[:, 4:6].unsqueeze(2).to_broadcast([P, ST, EXP]), ALU.is_le))
            link(TT(ce, ce, eq, ALU.mult))
            link(TT(mask, gt, ce, ALU.add))
            nc.vector.tensor_copy(maskb, mask).then_inc(masks, 1)
            dve.wait_ge(exps, 2)
            link(TT(ex, ex, mask, ALU.mult))
            link(nc.vector.tensor_reduce(rs1[:, 6:8], ex, AX_X, ALU.add))
            link(nc.vector.reciprocal(rs1[:, 8:10], rs1[:, 6:8]))
            link(TT(comb, ex, rs1[:, 8:10].unsqueeze(2).to_broadcast([P, ST, EXP]), ALU.mult))
            dve.wait_ge(count_mm, 1)
            link(nc.vector.tensor_scalar(posm, mask, -BIG, BIG, ALU.mult, ALU.add))
            link(TT(posm, posm, ps[:, 1, 0:ST * EXP].rearrange("p (c e) -> p c e", e=EXP), ALU.add))
            cnt, nb = rs1[0:EXP, 10:11], rs1[0:EXP, 11:12]
            link(nc.vector.tensor_copy(cnt, ps[0:EXP, 2, 0:1]))
            link(nc.vector.tensor_scalar(nb, cnt, float(BS), 1.0, ALU.is_gt, ALU.add))
            for b in range(2, S // BS):
                link(nc.vector.scalar_tensor_tensor(nb, cnt, float(BS * b), nb, ALU.is_gt, ALU.add))
            nc.vector.engine_nop().then_inc(pos_ready, 1)
            dve.wait_ge(plan_tr, 1)
            link(nc.vector.tensor_copy(pcT, ps[0:EXP, 3, :].rearrange("p (a t) -> p a t", t=P)))
            link(nc.vector.tensor_copy(rs1[0:EXP, 12:13], ps[0:EXP, 0, 0:1]))
            link(nc.vector.tensor_copy(blk_until[:, :], ps[0:1, 1, 0:EXP]))
            link(nc.vector.tensor_scalar(blk_last[:, :], ps[0:1, 1, 0:EXP], -1.0, None, ALU.add))
            link(nc.vector.tensor_scalar(cmp, blks[0:EXP, :], rs1[0:EXP, 12:13], None, ALU.is_ge))
            link(nc.vector.tensor_scalar(nbb, ones[0:EXP, :], nb, None, ALU.mult))
            nc.vector.engine_nop().then_inc(plan_cols, 1)
            dve.wait_ge(plan_mm, 1)
            link(nc.vector.tensor_scalar(bk, ps[:, 2, 0:NBC], pmod[:, :], None, ALU.is_equal))
            nc.vector.engine_nop().then_inc(plan_rows, 1)
            link(nc.vector.tensor_copy(blk_expert[:, :], ps[0:1, 2, 0:NBC]))
            link(TT(off, blks, ps[:, 2, 64:64 + NBC], ALU.subtract))
            link(nc.vector.tensor_scalar(off, off, float(BS), None, ALU.mult))
            dve.wait_ge(plan_sel, 1)
            sel = ps[:, 1, 0:4 * NBC].rearrange("p (a b) -> p a b", b=NBC)
            link(TT(blkcol[:, 0:2, :], sel[:, 0:2, :], off.unsqueeze(1).to_broadcast([P, 2, NBC]), ALU.subtract))
            link(nc.vector.tensor_copy(blkcol[:, 2:4, :], sel[:, 2:4, :]))
            nc.vector.engine_nop().then_inc(plan, 1)

            def ebias_for(i):
                for h in range(2):
                    ins = nc.vector.tensor_copy(ebias[:, h, 64 * h:64 * h + 64], bk[:, bass.ds(i, 1)].to_broadcast([P, BS]))
                return ins

            def onehot_for():
                for c in range(ST):
                    ins = nc.vector.tensor_scalar(onehot[:, c, :], slots[:, 0, :], cur[:, c:c + 1], None, ALU.is_equal)
                return ins

            link(nc.vector.tensor_copy(cur, blkcol[:, :, 0]))
            link(onehot_for())
            link(ebias_for(0))
            nc.vector.engine_nop().then_inc(onehot_ready, 1)
            nc.vector.engine_nop().then_inc(blk_step, 1)
            total = dve.value_load(blk_until[0:1, EXP - 1:EXP], min_val=EXP, max_val=NBLK)
            with dve.Fori(0, NBLK) as i:
                with dve.If(i < total):
                    dve.wait_ge(onehot_ready, i + 1)
                    for c in range(ST):
                        ins = nc.vector.tensor_scalar(wsel[:, c, :], slots.rearrange("p a b -> p (a b)"), cur[:, c:c + 1],
                                                      cur[:, 2 + c:3 + c], ALU.is_equal, ALU.mult)
                    ins.then_inc(wsel_ready, 1)
                    dve.wait_ge(wsel_ready, i + 1)
                    nc.vector.tensor_copy(cur, blkcol[:, :, bass.ds(i + 1, 1)].rearrange("p a b -> p (a b)")
                                          ).then_inc(blk_step, 1)
                    dve.wait_ge(blk_step, i + 2)
                    dve.wait_ge(gather_mm, i + 1)
                    dve.wait_ge(gu_done, i * KT + 1)
                    ebias_for(i + 1)
                    onehot_for().then_inc(onehot_ready, 1)
                    dve.wait_ge(gu_done, i * KT + KT)
                    nc.vector.tensor_scalar(g1, ps[:, 0, :], LIMIT, None, ALU.min).then_inc(g1_ready, 1)
                    nc.vector.tensor_scalar(l1, ps[:, 1, :], LIMIT, -LIMIT, ALU.min, ALU.max).then_inc(l1_ready, 1)
                    dve.wait_ge(g1_ready, i + 1)
                    dve.wait_ge(l1_ready, i + 1)
                    nc.vector.scalar_tensor_tensor(l1, l1, 1.0, g1, ALU.add, ALU.mult).then_inc(m_ready, 1)
                    dve.wait_ge(m_ready, i + 1)
                    dve.wait_ge(sg_ready, i + 1)
                    nc.vector.tensor_tensor(l1, l1, sg, ALU.mult).then_inc(act_ready, 1)
                    dve.wait_ge(sel_tr, i + 1)
                    nc.vector.tensor_copy(selT[0:64, 0, :], ps[0:64, 1, 0:S])
                    nc.vector.tensor_copy(selT[64:128, 1, :], ps[64:128, 1, 0:S]).then_inc(selT_ready, 1)
            dve.wait_ge(scattered, total + 1)
            for c in range(ST):
                link(TT(h2[:, c, :], h2[:, c, :], ps[:, 4 + 2 * c:6 + 2 * c, :].rearrange("p a b -> p (a b)"), ALU.add))
                nc.vector.engine_nop().then_inc(h2_ready, 1)
            dve.wait_ge(sumsq, 5)
            nc.vector.tensor_scalar(ss[:, 6:8], ss[:, 0:2], 1.0 / D, EPS_RMS, ALU.mult, ALU.add).then_inc(ms_ready, 1)
            dve.wait_ge(root, 3)
            rsqrt(2)
            for c in range(ST):
                nc.vector.scalar_tensor_tensor(h2[:, c, :], h2[:, c, :], ss[:, 12 + c:13 + c], gfin, ALU.mult,
                                               ALU.mult).then_inc(h2_ready, 1)

        @block.tensor
        def _(pe):
            pe.wait_ge(consts, 7)
            pe.wait_ge(par_in, 16 * 13)
            nc.tensor.transpose(ps[:, 7, 0:24], rows1, ident[0:24, 0:24]).then_inc(par_tr, 1)
            nc.tensor.transpose(ps[:, 7, 32:32 + TAPS * MT], rows2, ident[0:TAPS * MT, 0:TAPS * MT]).then_inc(par_tr, 1)
            pe.wait_ge(disc_rows, 1)
            for c in range(4):
                ins = nc.tensor.transpose(ps[:, 6, NB * c:NB * c + NB], arow[:, c, :], ident[0:NB, 0:NB])
            ins.then_inc(disc_tr, 1)
            pe.wait_ge(normed, 3)
            for k in range(KT):
                if k >= 4:
                    pe.wait_ge(h_dve if k % 2 == 0 else h_act, (k - 4) // 2 + 1)
                b = ps[:, k % 4, :]
                nc.tensor.transpose(b[:, 0:META], xin[0:META, 2, k * P:(k + 1) * P], ident[0:META, 0:META])
                nc.tensor.transpose(b[:, META:META + P], xin[:, 0, k * P:(k + 1) * P], ident[:, :])
                nc.tensor.transpose(b[:, META + P:L], xin[:, 1, k * P:(k + 1) * P], ident[:, :]).then_inc(h_tr, 1)
            pe.wait_ge(h_dve, 4)
            pe.wait_ge(h_act, 4)

            def z_tile(z):
                ld = z // 2
                if z % 2 == 0:
                    pe.wait_ge(slot_in[ld % MSLOT], 16 * (ld // MSLOT + 1))
                if z >= 4:
                    emptied(pe, z - 4)
                w = slot(ld, (KT, 256))
                n0 = 0 if z < 12 else META
                for k in range(KT):
                    ins = nc.tensor.matmul(ps[:, z % 4, 0:L - n0], w[:, k, (z % 2) * P:(z % 2) * P + P], hT[:, k, n0:L],
                                           start=(k == 0), stop=(k == KT - 1))
                ins.then_inc(mm, 1)

            def drives(q):
                pe.wait_ge(bz_ready, q + 1)
                for j in range(QB):
                    for ri in range(2):
                        n = 8 * q + 2 * j + ri
                        if n >= 2:
                            pe.wait_ge(drive_sb, n - 1)
                        else:
                            pe.wait_ge(bc_cols, 2)
                        nc.tensor.matmul(ps[:, 4 + ri, 0:L], bz[:, ri, j, :], uT[:, q, :], start=True, stop=True
                                         ).then_inc(drive_mm, 1)

            def outputs(q):
                pe.wait_ge(states, q + 1)
                if q:
                    pe.wait_ge(y_pre, q)
                for ri in range(2):
                    for j in range(QB):
                        ins = nc.tensor.matmul(ps[32 * j:32 * j + 32, 6, 0:S], cT[:, ri, q, 32 * j:32 * j + 32],
                                               prod[:, q % 2, ri, j, :], start=(ri == 0), stop=(ri == 1),
                                               tile_position=(0, 32 * j))
                ins.then_inc(y_mm, 1)

            def conv(n):
                m = MT - 1 - n
                pe.wait_ge(taps_ready, n + 1)
                pe.wait_ge(glu, 1)
                if n:
                    pe.wait_ge(conv_sb, n)
                for j in range(TAPS):
                    ins = nc.tensor.matmul(ps[:, 7, 0:S], taps[:, j, :], cin[:, m, j:j + S], start=(j == 0),
                                           stop=(j == TAPS - 1))
                ins.then_inc(conv_mm, 1)

            for z in range(8):
                z_tile(z)
            pe.wait_ge(bc_ready, 1)
            for ri in range(2):
                for q in range(MT):
                    nc.tensor.transpose(ps[:, 4 + ri, q * P:(q + 1) * P],
                                        bq[:, ri, q * QB:(q + 1) * QB, :, :].rearrange("p j g h -> p (j g h)"),
                                        ident[:, :]).then_inc(bc_tr, 1)
                    nc.tensor.transpose(ps[:, 6 + ri, q * P:(q + 1) * P],
                                        cq[:, ri, q, :, :].rearrange("p g s -> p (g s)"), ident[:, :]
                                        ).then_inc(bc_tr, 1)
            drives(0)
            for z in range(8, 12):
                z_tile(z)
            drives(1)
            for z in range(12, 16):
                z_tile(z)
            drives(2)
            conv(0)
            outputs(0)
            for z in range(16, 20):
                z_tile(z)
            drives(3)
            conv(1)
            outputs(1)
            for z in range(20, 24):
                z_tile(z)
            outputs(2)
            for z in range(24, 2 * N_IN):
                z_tile(z)
            outputs(3)
            pe.wait_ge(ya_ready, MT)
            for n in range(KT):
                for g in range(2):
                    ld = N_IN + 2 * (n // 4) + g
                    use = S5_USE + 2 * n + g
                    if n % 4 == 0:
                        pe.wait_ge(slot_in[ld % MSLOT], 16 * (ld // MSLOT + 1))
                    emptied(pe, use - 4)
                    w = slot(ld, (MT, 512))
                    for k in range(MT):
                        ins = nc.tensor.matmul(ps[:, use % 4, 0:S], w[:, k, (n % 4) * P:(n % 4) * P + P], ya[:, k, :],
                                               start=(k == 0), stop=(k == MT - 1))
                    ins.then_inc(mm, 1)
                if n == 1:
                    pe.wait_ge(conv_done, 1)
                    pe.wait_ge(conv_sb, PE_TILES)
                    for m in range(MT):
                        ins = nc.tensor.matmul(ps[:, 7, 0:S], invc[:, :], cacc[:, m, :], start=(m == 0),
                                               stop=(m == MT - 1))
                    ins.then_inc(mean_mm, 1)
                if n == 3:
                    pe.wait_ge(squared, 1)
                    for m in range(MT):
                        ins = nc.tensor.matmul(ps[:, 7, S:2 * S], invc[:, :], csq[:, m, :], start=(m == 0),
                                               stop=(m == MT - 1))
                    ins.then_inc(var_mm, 1)
            pe.wait_ge(conv_act, MT)
            for n in range(KT):
                ld, use = N_IN + 4 + n // 4, CO_USE + n
                if n % 4 == 0:
                    pe.wait_ge(slot_in[ld % MSLOT], 16 * (ld // MSLOT + 1))
                emptied(pe, use - 4)
                w = slot(ld, (MT, 512))
                for k in range(MT):
                    ins = nc.tensor.matmul(ps[:, use % 4, 0:S], w[:, k, (n % 4) * P:(n % 4) * P + P], cacc[:, k, :],
                                           start=(k == 0), stop=(k == MT - 1))
                ins.then_inc(mm, 1)
            pe.wait_ge(merge_ready, KT + 1)
            for k in range(KT):
                ld = N_IN + 6 + k // 2
                if k % 2 == 0:
                    pe.wait_ge(slot_in[ld % MSLOT], 16 * (ld // MSLOT + 1))
                w = slot(ld, (2, 1024))
                for c in range(ST):
                    for h in range(2):
                        ins = nc.tensor.matmul(ps[:, (WO_USE + 2 * c + h) % 4, :], merged[:, k, c * P:(c + 1) * P],
                                               w[:, k % 2, 512 * h:512 * h + 512], start=(k == 0), stop=(k == KT - 1))
                        if k == KT - 1:
                            ins.then_inc(mm, 1)
                if k % 2 and k < KT - 1:
                    ins.then_inc(wo_used, 1)
            pe.wait_ge(hf_ready, 3)
            for b in range(4):
                for kk in range(2):
                    for c in range(ST):
                        k = 2 * b + kk
                        ins = nc.tensor.transpose(ps[:, 4 + b, kk * S + c * P:kk * S + c * P + P],
                                                  hf[:, c, k * P:(k + 1) * P], ident[:, :])
                ins.then_inc(hf_tr, 1)
            pe.wait_ge(hfT_act, 2)
            pe.wait_ge(hfT_dve, 2)
            pe.wait_ge(h2_ready, 2)
            for c in range(ST):
                for k in range(KT):
                    ins = nc.tensor.matmul(ps[:, 0, c * EXP:(c + 1) * EXP], hfT[:, k, c * P:(c + 1) * P], rw[:, k, :],
                                           start=(k == 0), stop=(k == KT - 1))
            ins.then_inc(logit_mm, 1)
            pe.wait_ge(masks, 1)
            nc.tensor.matmul(ps[:, 1, 0:EXP], upper, maskb[:, 0, :], start=True, stop=True)
            nc.tensor.matmul(ps[:, 1, EXP:2 * EXP], onesb, maskb[:, 0, :], start=True, stop=False)
            nc.tensor.matmul(ps[:, 1, EXP:2 * EXP], upper, maskb[:, 1, :], start=False, stop=True)
            for c in range(ST):
                ins = nc.tensor.matmul(ps[0:EXP, 2, 0:1], maskb[:, c, :], onesb[:, 0:1], start=(c == 0), stop=(c == 1))
            ins.then_inc(count_mm, 1)
            pe.wait_ge(pos_ready, 1)
            for a, t in enumerate((posm, comb)):
                for c in range(ST):
                    nc.tensor.transpose(ps[0:EXP, 3, (2 * a + c) * P:(2 * a + c + 1) * P], t[:, c, :], ident[:, :])
            nb = rs1[0:EXP, 11:12]
            nc.tensor.matmul(ps[0:EXP, 0, 0:1], tri, nb, start=True, stop=True)
            nc.tensor.matmul(ps[0:1, 1, 0:EXP], nb, tri, start=True, stop=True).then_inc(plan_tr, 1)
            pe.wait_ge(plan_cols, 1)
            nc.tensor.matmul(ps[:, 2, 0:NBC], ones[0:EXP, :], cmp, start=True, stop=True)
            nc.tensor.matmul(ps[:, 2, 64:64 + NBC], nbb, cmp, start=True, stop=True).then_inc(plan_mm, 1)
            pe.wait_ge(plan_rows, 1)
            for a in range(4):
                ins = nc.tensor.matmul(ps[:, 1, a * NBC:(a + 1) * NBC], pcT[:, a, :], bk[0:EXP, :], start=True, stop=True)
            ins.then_inc(plan_sel, 1)
            pe.wait_ge(late_in, 16 * 8)
            for c in range(ST):
                for h in range(2):
                    nc.tensor.matmul(ps[:, 4 + 2 * c + h, :], pcT[:, 2 + c, :], bdown[:, 512 * h:512 * h + 512],
                                     start=True, stop=False, skip_group_check=True)

            def gather():
                for k in range(KT):
                    for c in range(ST):
                        for part in range(3):
                            ins = nc.tensor.matmul(ps[:, 3, k * BS:(k + 1) * BS], hp[:, part, c, k * P:(k + 1) * P],
                                                   onehot[:, c, :], start=(c == 0 and part == 0),
                                                   stop=(c == 1 and part == 2))
                return ins

            def scatter():
                for c in range(ST):
                    for h in range(2):
                        ins = nc.tensor.matmul(ps[:, 4 + 2 * c + h, :], selT[:, h, c * P:(c + 1) * P], ysb,
                                               start=False, stop=False, skip_group_check=True)
                return ins

            pe.wait_ge(parts, 1)
            pe.wait_ge(onehot_ready, 1)
            gather().then_inc(gather_mm, 1)
            pe.wait_ge(late_consts, 6)
            total = pe.value_load(blk_until[0:1, EXP - 1:EXP], min_val=EXP, max_val=NBLK)
            with pe.Fori(0, NBLK) as i:
                with pe.If(i < total):
                    e = pe.value_load(blk_expert[0:1, bass.ds(i, 1)], min_val=0, max_val=EXP)
                    pe.wait_ge(selT_ready, i + 1)
                    for a in range(2):
                        for h in range(2):
                            nc.tensor.matmul(ps[:, a, :], ebias[0:96, h, :], bp[:, a * D + 512 * h:a * D + 512 * h + 512],
                                             start=(h == 0), stop=False, skip_group_check=True)
                    pe.wait_ge(xT_ready, i + 1)
                    for k in range(KT):
                        pe.wait_ge(gu_in[k], e * 16 + 16)
                        for a in range(2):
                            for h in range(2):
                                ins = nc.tensor.matmul(ps[64 * h:64 * h + 64, a, :], xT[:, k, :], gsl[k][:, 2 * a + h, :],
                                                       start=False, stop=(k == KT - 1), skip_group_check=True,
                                                       tile_position=(0, 64 * h))
                        ins.then_inc(gu_done, 1)
                    pe.wait_ge(y_ready, i + 1)
                    scatter().then_inc(scattered, 1)
                    pe.wait_ge(onehot_ready, i + 2)
                    gather().then_inc(gather_mm, 1)
                    pe.wait_ge(act_ready, i + 1)
                    for j in range(4):
                        ins = nc.tensor.transpose(ps[:, 0, j * P:(j + 1) * P], l1[:, j * P:(j + 1) * P], ident[:, :])
                    ins.then_inc(act_tr, 1)
                    pe.wait_ge(wsel_ready, i + 1)
                    for c in range(ST):
                        ins = nc.tensor.transpose(ps[:, 1, c * P:(c + 1) * P], wsel[:, c, :], ident[:, :])
                    ins.then_inc(sel_tr, 1)
                    pe.wait_ge(actT_ready, i + 1)
                    for k in range(KT):
                        pe.wait_ge(dn_in[k], e * 16 + 16)
                        for h in range(2):
                            ins = nc.tensor.matmul(ps[64 * h:64 * h + 64, 2, :], actT[:, k % 4, 64 * (k // 4):64 * (k // 4) + 64],
                                                   dsl[k][:, h, :], start=(k == 0), stop=(k == KT - 1),
                                                   skip_group_check=True, tile_position=(0, 64 * h))
                        ins.then_inc(dn_done, 1)
            pe.wait_ge(y_ready, total + 1)
            pe.wait_ge(selT_ready, total + 1)
            scatter().then_inc(scattered, 1)


_INS = ["x", "meta_tokens", "norm_mix_g", "w_in", "ssm_a_re", "ssm_a_im", "ssm_log_dt", "ssm_b_re", "ssm_b_im",
        "ssm_c_re", "ssm_c_im", "ssm_d", "w_s5_lin", "w_s5_gate", "conv_dw_w", "conv_dw_b", "conv_ln_g", "conv_ln_b",
        "w_conv_out", "w_out", "norm_ffn_g", "router_w", "router_b", "w_gate_up", "b_gate_up", "w_down", "b_down",
        "norm_final_g"]


def kernel(**inputs):
    import concourse.bacc as bacc
    from concourse.bass_utils import run_bass_kernel_spmd as run

    nc = bacc.Bacc("TRN2", target_bir_lowering=False, num_devices=1)
    arrays, aps = {}, {}
    for name in _INS:
        a = np.ascontiguousarray(inputs[name])
        arrays[f"in_{name}"] = a
        aps[name] = nc.dram_tensor(f"in_{name}", a.shape, mybir.dt.from_np(a.dtype), kind="ExternalInput").ap()
    out = nc.dram_tensor("out", (1, S, D), F32, kind="ExternalOutput").ap()
    build(nc, aps, out)
    r = run(nc, [arrays], core_ids=[0])
    return r.results[0]["out"]
```

```python
from contextlib import ExitStack

import numpy as np

import concourse.bass as bass
from concourse import mybir

F32 = mybir.dt.float32
BF16 = mybir.dt.bfloat16
I32 = mybir.dt.int32
ALU = mybir.AluOpType
ACT = mybir.ActivationFunctionType
AX_X = mybir.AxisListType.X

P = 128
D = 1024
KT = D // P
S = 256
ST = S // P
META = 16
L = S + META
DS = D // 2
MT = DS // P
NB = 16
QB = NB // MT
TAPS = 31
HALO = TAPS - 1 - META
EXP = 32
TOPK = 4
BS = 64
NBLK = EXP + (S * TOPK) // BS - 1
NBC = NBLK + 1
AHEAD = 3
TURNS = 5
EPS_RMS, EPS_LN = 1e-6, 1e-5
LIMIT, ALPHA = 7.0, 1.702
SLOT = 2048
NSLOT = 12
MSLOT = 8
SH = 4
TG = (TAPS + SH - 1) // SH
CW = HALO + L + 2
XW = S + SH * (TG - 1)
MAGIC = 1.5 * 2.0 ** 23
TWO_PI = (6.28125, 0.0019350051879882812, 3.0199159819567e-07)
LN2 = (0.693359375, -2.12194440e-4)
BIG = 9999.0


def build(nc, T, out):
    with ExitStack() as ctx:
        def sb(name, shape, dt=F32):
            return ctx.enter_context(nc.sbuf_tensor(name, shape, dt))

        def sem(name):
            return ctx.enter_context(nc.semaphore(name))

        Y_AT = NSLOT * SLOT
        G_AT = Y_AT + MT * S
        B_AT = G_AT + QB * L
        A_AT = B_AT + KT * L
        ring = sb("ring", [P, A_AT + 4096])
        rY, rG, rB, rA = (ring, Y_AT), (ring, G_AT), (ring, B_AT), (ring, A_AT)
        rC = sb("rC", [P, 4096])
        rD = sb("rD", [P, 3 * QB * L])
        rE = sb("rE", [P, 2 * QB * L])
        rF = sb("rF", [P, 2 * QB * L])
        rX = sb("rX", [P, 2048])
        rU = sb("rU", [P, MT * L])
        rP = sb("rP", [P, MT * CW])
        rQ = sb("rQ", [P, MT * L])
        rW = sb("rW", [P, 1024])

        def view(r, at, *dims, rows=P, dt=F32):
            n = 1
            for d in dims:
                n *= d
            words = n // 2 if dt == BF16 else n
            if isinstance(r, tuple):
                r, at = r[0], r[1] + at
            v = r[0:rows, at:at + words]
            if dt != F32:
                v = v.bitcast(dt)
            if len(dims) == 2:
                v = v.rearrange("p (a b) -> p a b", b=dims[1])
            if len(dims) == 3:
                v = v.rearrange("p (a b c) -> p a b c", b=dims[1], c=dims[2])
            if len(dims) == 4:
                v = v.rearrange("p (a b c d) -> p a b c d", b=dims[1], c=dims[2], d=dims[3])
            return v

        xin = view(rA, 0, 3, D)
        junk = view(rA, 3072, D)
        hT = view(rB, 0, KT, L)
        gates = view(rC, 0, 2 * KT, S)
        work = MSLOT * SLOT
        cosT = [view(rD, 0, QB, L), view(ring, work, QB, L)]
        sinT = [view(rD, QB * L, QB, L), view(ring, work + QB * L, QB, L)]
        tabtmp = view(rD, 2 * QB * L, QB, L)
        phase = view(rD, 2 * QB * L, NB, 33)
        drive = view(rE, 0, 2, QB, L)
        rot = view(rF, 0, 2, QB, L)
        rtmp = view(rG, 0, QB, L)
        wtap = view(ring, work + 2 * QB * L, TG, MT, 32)
        shifted = view(ring, work + 2 * QB * L + 1024, MT, MT, XW)
        prod = view(rA, 0, 2, 2, QB, S)
        uT = view(rU, 0, MT, L)
        cin = view(rP, 0, MT, CW)
        cgate = view(rQ, 0, MT, L)
        cacc = view(rQ, 0, MT, S)
        ya = view(rY, 0, MT, S)
        merged = view(rB, 0, KT, S)
        csq = view(rE, 0, MT, S)
        lnr = view(rE, 1024, S)
        lnt = view(rE, 1280, S)
        lnv = view(rE, 1536, S)
        sig = view(rG, 0, 2, S)
        mtmp = view(rG, 512, 2, S)
        bq = view(rE, 0, 2, NB, 2, 16)
        cq = view(rE, 1024, 2, MT, 2, 64)
        bn = view(rF, 0, 2, NB, 16)
        cn = view(rF, 512, 2, MT, 64)
        pt1 = view(rF, 1024, NB, 16)
        pt2 = view(rF, 1280, NB, 16)
        bT = view(rX, 0, 2, MT, P)
        bz = view(rX, 1024, 2, QB, P)
        cT = view(rW, 0, 2, MT, P)
        h2 = view(rX, 0, ST, D)
        gffn = view(rF, 0, D)
        gfin = view(rF, D, D)
        rw = view(rU, 0, KT, EXP)
        rb = view(rU, 256, EXP)
        bgu = view(rA, 0, 2 * D, rows=96)
        bg2 = view(rA, 2048, 2 * D, rows=96, dt=BF16)
        bp = view(rW, 0, 2 * D, rows=96, dt=BF16)
        hf = view(rA, 0, ST, D)
        hr = view(rA, 2048, ST, D)
        h2T = view(rD, 0, KT, S)
        hp = view(rC, 0, 3, ST, D, dt=BF16)
        g1 = view(rD, 0, 512)
        l1 = view(rD, 512, 512)
        sg = view(rD, 1024, 512)
        actT = view(rD, 1536, 4, P)
        ysb = view(rD, 2048, 512)
        xT = view(rD, 2560, KT, BS)
        upper = view(rP, 0, P, dt=BF16)
        onesb = view(rP, 64, P, dt=BF16)
        slots = view(rE, 1880, 2, BS)
        blks = view(rE, 2008, NBC)
        tri = view(rE, 2056, EXP, rows=EXP)
        onehot = view(rE, 0, ST, BS, dt=BF16)
        wsel = view(rE, 64, ST, P)
        selT = view(rE, 320, 2, S)
        ebias = view(rE, 832, 2, P, dt=BF16)
        blkcol = view(rE, 960, 4, NBC)
        bk = view(rE, 1152, NBC)
        lg = view(rE, 1200, ST, EXP)
        gt = view(rE, 1264, ST, EXP)
        eq = view(rE, 1328, ST, EXP)
        ce = view(rE, 1392, ST, EXP)
        mask = view(rE, 1456, ST, EXP)
        ex = view(rE, 1520, ST, EXP)
        comb = view(rE, 1584, ST, EXP)
        posm = view(rE, 1648, ST, EXP)
        maskb = view(rE, 1712, ST, EXP, dt=BF16)
        cmp = view(rE, 1744, NBC, rows=EXP)
        off = view(rE, 1792, NBC)
        v8 = view(rE, 1840, ST, 8)
        rs1 = view(rE, 1856, 16)
        cur = view(rE, 1872, 4)
        pcT = view(rQ, 0, 4, P, rows=EXP)
        nbb = view(rQ, 512, P, rows=EXP)
        ident = sb("ident", [P, P])
        ones = sb("ones", [P, P])
        invc = sb("invc", [P, P])
        seg = sb("seg", [P, 8])
        pidx = sb("pidx", [P, 1])
        expo = sb("expo", [P, 17])
        hmask = sb("hmask", [P, 2])
        jmask = sb("jmask", [P, 4])
        pmod = sb("pmod", [P, 1])
        rT = sb("rT", [P, 2 * NB * 33])
        es = view(rT, 0, NB, 33)
        ec = view(rT, NB * 33, NB, 33)
        colp = sb("colp", [P, 32])
        cw = sb("cw", [P, TG, MT * MT])
        sel32 = sb("sel32", [P, 32])
        rows1 = view(rG, 0, P, rows=32)
        rows2 = view(rG, 128, P)
        arow = view(rG, 256, 4, P, rows=NB)
        ldt = view(rG, 768, 2, rows=NB)
        dts = view(rG, 770, 2, rows=NB)
        xs = view(rG, 780, 6, 16)
        pc = sb("pc", [P, 4, NB])
        sp_ = sb("sp_", [P, 6, NB])
        xi = sb("xi", [P, NB], I32)
        ss = sb("ss", [P, 16])
        blk_expert = sb("blk_expert", [1, NBC], I32)
        blk_odd = sb("blk_odd", [1, NBC], I32)
        blk_until = sb("blk_until", [1, EXP], I32)
        blk_last = sb("blk_last", [1, EXP], I32)
        decay, abr, abi, den, cre, cim = (sp_[:, n, :] for n in range(6))

        ps = ctx.enter_context(nc.psum_tensor("ps", [P, 8, 512], F32))

        x_in = [sem(f"x_in{n}") for n in range(3)]
        par_in, xres_in, late_in = sem("par_in"), sem("xres_in"), sem("late_in")
        slot_in = [sem(f"slot_in{n}") for n in range(MSLOT)]
        gu_even = [sem(f"gu_even{n}") for n in range(KT)]
        gu_in = [gu_even, [sem(f"gu_odd{n}") for n in range(AHEAD)] + gu_even[AHEAD:]]
        dn_in = [[sem(f"dn_{name}{n}") for n in range(KT)] for name in ("even", "odd")]
        pool_step, consts, tables, late_consts = sem("pool_step"), sem("consts"), sem("tables"), sem("late_consts")
        dve_step, act_step = sem("dve_step"), sem("act_step")
        sumsq, ms_ready, root, normed = sem("sumsq"), sem("ms_ready"), sem("root"), sem("normed")
        h_tr, h_act, h_dve = sem("h_tr"), sem("h_act"), sem("h_dve")
        par_tr, par_cols, disc_rows = sem("par_tr"), sem("par_cols"), sem("disc_rows")
        disc_tr, phases, sines, etab = sem("disc_tr"), sem("phases"), sem("sines"), sem("etab")
        bc_ready, bc_tr, bc_cols = sem("bc_ready"), sem("bc_tr"), sem("bc_cols")
        bz_ready, drive_mm, drive_sb, drive_used = sem("bz_ready"), sem("drive_mm"), sem("drive_sb"), sem("drive_used")
        tab_used, states, y_mm, y_pre, ya_ready = (sem("tab_used"), sem("states"), sem("y_mm"), sem("y_pre"),
                                                   sem("ya_ready"))
        mm, mm_act, mm_dve, wo_used = sem("mm"), sem("mm_act"), sem("mm_dve"), sem("wo_used")
        glu, mean_mm, centred, squared, var_mm = (sem("glu"), sem("mean_mm"), sem("centred"), sem("squared"),
                                                  sem("var_mm"))
        var_ready, ln_root, ln_ready, conv_act = sem("var_ready"), sem("ln_root"), sem("ln_ready"), sem("conv_act")
        merge_ready, h2_ready, hf_ready = sem("merge_ready"), sem("h2_ready"), sem("hf_ready")
        h2T_act, h2T_dve, part1, rest1, part2, parts = (sem("h2T_act"), sem("h2T_dve"), sem("part1"), sem("rest1"),
                                                        sem("part2"), sem("parts"))
        logit_mm, top1, exps, masks, count_mm, pos_ready = (sem("logit_mm"), sem("top1"), sem("exps"), sem("masks"),
                                                            sem("count_mm"), sem("pos_ready"))
        plan_tr, plan_cols, plan_mm, plan_sel, plan = (sem("plan_tr"), sem("plan_cols"), sem("plan_mm"),
                                                       sem("plan_sel"), sem("plan"))
        onehot_ready, gather_mm, xT_ready = sem("onehot_ready"), sem("gather_mm"), sem("xT_ready")
        gu_done, dn_done, g1_ready, sg_ready, act_ready = (sem("gu_done"), sem("dn_done"), sem("g1_ready"),
                                                           sem("sg_ready"), sem("act_ready"))
        wsel_ready, act_tr, sel_tr, actT_ready, selT_ready = (sem("wsel_ready"), sem("act_tr"), sem("sel_tr"),
                                                              sem("actT_ready"), sem("selT_ready"))
        y_ready, scattered, blk_step, l1_ready, m_ready = (sem("y_ready"), sem("scattered"), sem("blk_step"),
                                                           sem("l1_ready"), sem("m_ready"))
        stored, bq_zero, bgu_in, rw_in, bias_parts = (sem("stored"), sem("bq_zero"), sem("bgu_in"), sem("rw_in"),
                                                      sem("bias_parts"))
        result, gated, rw_ready, h2_tr, wo_mm, final_sum = (sem("result"), sem("gated"), sem("rw_ready"),
                                                            sem("h2_tr"), sem("wo_mm"), sem("final_sum"))
        taps_ready, conv_mm, conv_sb, tap_in, shifts, cw_ready = (sem("taps_ready"), sem("conv_mm"), sem("conv_sb"),
                                                                  sem("tap_in"), sem("shifts"), sem("cw_ready"))
        scales = sem("scales")
        rows_in, bc_in, times_g = sem("rows_in"), sem("bc_in"), sem("times_g")
        blocks_ready, pc_tr, bdown_in = sem("blocks_ready"), sem("pc_tr"), sem("bdown_in")

        w_in = T["w_in"][0].rearrange("(k p) n -> p k n", p=P)
        s5l = T["w_s5_lin"][0].rearrange("(k p) n -> p k n", p=P)
        s5g = T["w_s5_gate"][0].rearrange("(k p) n -> p k n", p=P)
        wco = T["w_conv_out"][0].rearrange("(k p) n -> p k n", p=P)
        wout = T["w_out"][0].rearrange("(k p) n -> p k n", p=P)
        in_cols = [0, 256, 512, 1024, 768, 1280] + [DS + 2 * DS + 256 * n for n in range(8)]
        loads = [w_in[:, :, c:c + 256] for c in in_cols]
        loads += [s5l[:, :, 0:512], s5g[:, :, 0:512], s5l[:, :, 512:1024], s5g[:, :, 512:1024]]
        loads += [wco[:, :, 0:512], wco[:, :, 512:1024]]
        loads += [wout[:, 2 * n:2 * n + 2, :] for n in range(4)]
        N_IN, N_LOADS = len(in_cols), len(loads)

        PE_ORDER = []
        between = {9: [("drives", 0)], 12: [("drives", 1)], 15: [("conv", 0), ("outputs", 0)], 16: [("drives", 2)],
                   18: [("conv", 1), ("outputs", 1)], 20: [("drives", 3)], 22: [("conv", 2), ("outputs", 2)],
                   24: [("outputs", 3), ("conv", 3)], 25: [("mean", 0)], 26: [("gelu", 0)]}
        for z in range(8, 2 * N_IN):
            PE_ORDER += between.get(z, []) + [("z", z)]

        def slot(n, dims):
            return view(ring, (n % MSLOT) * SLOT, *dims)

        USES = ["act"] * (2 * N_IN) + ["dve"] * (2 * KT)
        S5_USE, CO_USE = 2 * N_IN, 2 * N_IN + KT

        def emptied(eng, use):
            who = USES[use]
            eng.wait_ge(mm_act if who == "act" else mm_dve, USES[:use + 1].count(who))

        def used_up(eng, n):
            if n < N_IN:
                eng.wait_ge(mm, 2 * n + 2)
            elif n < N_IN + 4:
                eng.wait_ge(mm, S5_USE + 4 * ((n - N_IN) // 2 + 1))
            elif n < N_IN + 6:
                eng.wait_ge(mm, CO_USE + 4 * (n - N_IN - 3))
            elif n < N_LOADS - 1:
                eng.wait_ge(wo_used, n - N_IN - 5)
            else:
                eng.wait_ge(wo_mm, 2 * ST)

        gsl = [[[view(ring, k * SLOT + a * 1024, 2, 512) for a in range(2)] for k in range(KT)] for odd in range(2)]
        gwhole = [view(ring, k * SLOT, 4, 512) for k in range(KT)]
        spare = [(rC, 3072), (rF, 0), (rU, 0), (rQ, 0), (rT, 0), (rP, P)]
        for k in range(AHEAD):
            gsl[1][k] = [view(*spare[2 * k + a], 2, 512) for a in range(2)]
        DN_AT, DN_ODD = KT * SLOT, KT * 1024
        dsl = [[view(ring, DN_AT + odd * DN_ODD + k * 1024, 2, 512) for k in range(KT)] for odd in range(2)]

        block = ctx.enter_context(nc.Block())

        @block.sync
        def _(sp):
            sp.dma_start(xin[0:P, 0, :], T["x"][0, 0:P, :]).then_inc(x_in[0], 16)
            sp.dma_start(xin[0:P, 1, :], T["x"][0, P:S, :]).then_inc(x_in[1], 16)
            def load(n):
                if n >= MSLOT:
                    used_up(sp, n - MSLOT)
                dims = (KT, 256) if n < N_IN else ((MT, 512) if n < N_LOADS - 4 else (2, 1024))
                sp.dma_start(slot(n, dims), loads[n]).then_inc(slot_in[n % MSLOT], 16)

            def first_gu(e, k):
                rows = T["w_gate_up"][0, e, k * P:(k + 1) * P, :]
                if k < AHEAD:
                    for a in range(2):
                        sp.dma_start(gsl[e][k][a], rows[:, a * D:(a + 1) * D].rearrange("p (a b) -> p a b", b=512)
                                     ).then_inc(gu_in[e][k], 16)
                else:
                    sp.dma_start(gwhole[k], rows.rearrange("p (a b) -> p a b", b=512)).then_inc(gu_in[e][k], 16)

            def first_dn(e, k):
                sp.dma_start(dsl[e][k], T["w_down"][0, e, k * P:(k + 1) * P, :].rearrange("p (a b) -> p a b", b=512)
                             ).then_inc(dn_in[e][k], 16)

            sp.dma_start(xin[0:META, 2, :], T["meta_tokens"]).then_inc(x_in[2], 16)
            sp.dma_start(ldt, T["ssm_log_dt"].rearrange("o (b g) -> (o b) g", g=2)).then_inc(par_in, 16)
            sp.dma_start(arow[:, 2, :], T["ssm_a_re"].rearrange("o (b g) p -> (o b) (g p)", g=2)).then_inc(par_in, 16)
            sp.dma_start(arow[:, 3, :], T["ssm_a_im"].rearrange("o (b g) p -> (o b) (g p)", g=2)).then_inc(par_in, 16)
            for name, at, n in (("norm_mix_g", 0, 8), ("ssm_d", 8, 4), ("conv_dw_b", 12, 4), ("conv_ln_g", 16, 4),
                                ("conv_ln_b", 20, 4), ("norm_ffn_g", 24, 8)):
                sp.dma_start(rows1[at:at + n, :], T[name].rearrange("o (m p) -> (o m) p", p=P)).then_inc(rows_in, 16)
            for n, (b, c) in enumerate((("ssm_b_re", "ssm_c_re"), ("ssm_b_im", "ssm_c_im"))):
                sp.dma_start(bn[:, n, :, :], T[b][0].rearrange("g p h -> (g p) h").rearrange("(b q) h -> q b h", q=P)
                             ).then_inc(bc_in, 16)
                sp.dma_start(cn[:, n, :, :], T[c][0].rearrange("g h p -> (g h) p").rearrange("(m q) p -> q m p", q=P)
                             ).then_inc(bc_in, 16)
            for n in range(4):
                load(n)
            dw = T["conv_dw_w"][0].rearrange("j o (q c) -> (j o) q c", c=32)
            for a in range(TG):
                h = min(SH, TAPS - SH * a)
                sp.dma_start(rows2[16 * a:16 * a + 16, 0:32 * h].rearrange("q (h c) -> q h c", c=32),
                             dw[SH * a:SH * a + h].rearrange("h q c -> q h c")).then_inc(tap_in, 16)
            sp.dma_start(rows2[16 * (TG - 1):16 * TG, 96:128], dw[TAPS - 1]).then_inc(tap_in, 16)
            for n in range(4, N_IN):
                load(n)
            sp.wait_ge(glu, 1)
            for g in range(MT):
                for h in range(SH):
                    sp.dma_start(shifted[32 * h:32 * h + 32, :, g, :], cin[32 * g:32 * g + 32, :, h:h + XW]
                                 ).then_inc(shifts, 16)
            for n in range(N_IN, N_IN + 6):
                load(n)
            sp.wait_ge(drive_mm, 8 * MT)
            sp.dma_start(h2[:, 0, :], T["x"][0, 0:P, :]).then_inc(xres_in, 16)
            sp.dma_start(h2[:, 1, :], T["x"][0, P:S, :]).then_inc(xres_in, 16)
            for n in range(N_IN + 6, N_IN + 8):
                load(n)
            sp.wait_ge(y_mm, MT)
            for c in range(3):
                sp.dma_start(bgu[32 * c:32 * c + 32, :], T["b_gate_up"][0]).then_inc(bgu_in, 16)
            sp.wait_ge(y_pre, MT)
            sp.dma_start(rw, T["router_w"][0].rearrange("(k p) e -> p k e", p=P)).then_inc(rw_in, 16)
            sp.dma_start(rb, T["router_b"][0:1, :].to_broadcast([P, EXP])).then_inc(rw_in, 16)
            sp.dma_start(gffn, T["norm_ffn_g"][0:1, :].to_broadcast([P, D])).then_inc(late_in, 16)
            sp.dma_start(gfin, T["norm_final_g"].rearrange("(a n) -> a n", a=1).to_broadcast([P, D])
                         ).then_inc(late_in, 16)
            sp.wait_ge(conv_mm, MT)
            for k in range(KT):
                first_dn(0, k)
            for n in range(N_IN + 8, N_LOADS):
                load(n)
            for k in range(KT):
                used_up(sp, 2 * MSLOT + k)
                first_gu(0, k)
            sp.wait_ge(y_ready, 1)
            for h in range(2):
                sp.dma_start(ysb[64 * h:64 * h + EXP, :], T["b_down"][0, :, 512 * h:512 * h + 512]
                             ).then_inc(bdown_in, 16)
            sp.wait_ge(wo_mm, 2 * ST)
            for k in range(4):
                first_dn(1, k)
            sp.wait_ge(parts, ST)
            for k in range(4, KT):
                first_dn(1, k)
            sp.wait_ge(plan, 1)
            sp.wait_ge(plan_sel, 1)
            for k in range(AHEAD):
                first_gu(1, k)

            def used_by(e):
                return sp.value_load(blk_last[0:1, bass.ds(e, 1)], min_val=0, max_val=NBLK - 1)

            def load_gu(e, odd, first, until, last):
                for k in range(first, until):
                    sp.wait_ge(gu_done, last * KT + (k + 1))
                    rows = T["w_gate_up"][0, bass.ds(e, 1), k * P:(k + 1) * P, :]
                    if k < AHEAD:
                        for a in range(2):
                            sp.dma_start(gsl[odd][k][a], rows[:, :, a * D:(a + 1) * D].rearrange(
                                "o p (a b) -> p (o a) b", b=512)).then_inc(gu_in[odd][k], 16)
                    else:
                        sp.dma_start(gwhole[k], rows.rearrange("o p (a b) -> p (o a) b", b=512)
                                     ).then_inc(gu_in[odd][k], 16)

            def load_dn(e, odd, last):
                for k in range(KT):
                    sp.wait_ge(dn_done, last * KT + (k + 1))
                    sp.dma_start(dsl[odd][k], T["w_down"][0, bass.ds(e, 1), k * P:(k + 1) * P, :].rearrange(
                        "o p (a b) -> p (o a) b", b=512)).then_inc(dn_in[odd][k], 16)

            with sp.Fori(0, EXP // 2 - 2) as j:
                for odd in range(2):
                    last = used_by(2 * j + odd)
                    load_gu(2 * j + odd + 1, 1 - odd, AHEAD, KT, last)
                    load_dn(2 * j + odd + 2, odd, last)
                    load_gu(2 * j + odd + 2, odd, 0, AHEAD, last)
            last = used_by(EXP - 4)
            load_gu(EXP - 3, 1, AHEAD, KT, last)
            load_dn(EXP - 2, 0, last)
            load_gu(EXP - 2, 0, 0, AHEAD, last)
            last = used_by(EXP - 3)
            load_gu(EXP - 2, 0, AHEAD, KT, last)
            load_gu(EXP - 1, 1, 0, AHEAD, last)
            load_gu(EXP - 1, 1, AHEAD, KT, used_by(EXP - 2))
            load_dn(EXP - 1, 1, last)
            for c in range(ST):
                sp.wait_ge(result, c + 1)
                sp.dma_start(out[0, c * P:(c + 1) * P, :], h2[:, c, :]).then_inc(stored, 16)
            sp.wait_ge(stored, 16 * ST)

        @block.gpsimd
        def _(pool):
            n = [0]

            def link(ins):
                n[0] += 1
                ins.then_inc(pool_step, 1)
                pool.wait_ge(pool_step, n[0])

            link(nc.gpsimd.memset(ident[:, :], 0.0))
            nc.gpsimd.affine_select(out=ident[:, :], in_=ident[:, :], compare_op=ALU.not_equal, fill=1.0, base=0,
                                    pattern=[[-1, P]], channel_multiplier=1).then_inc(consts, 1)
            nc.gpsimd.memset(ones[:, :], 1.0).then_inc(consts, 1)
            nc.gpsimd.memset(invc[:, :], 1.0 / DS).then_inc(consts, 1)
            nc.gpsimd.iota(pidx[:, :], pattern=[[0, 1]], base=0, channel_multiplier=1,
                           allow_small_or_imprecise_dtypes=True).then_inc(consts, 1)
            nc.gpsimd.iota(expo[:, :], pattern=[[1, 17]], base=0, channel_multiplier=0,
                           allow_small_or_imprecise_dtypes=True).then_inc(consts, 1)
            link(nc.gpsimd.memset(seg[:, :], 1.0))
            link(nc.gpsimd.affine_select(out=seg[:, :], in_=seg[:, :], compare_op=ALU.is_ge, fill=0.0, base=0,
                                         pattern=[[-16, 8]], channel_multiplier=1))
            nc.gpsimd.affine_select(out=seg[:, :], in_=seg[:, :], compare_op=ALU.is_ge, fill=0.0, base=15,
                                    pattern=[[16, 8]], channel_multiplier=-1).then_inc(consts, 1)
            nc.gpsimd.memset(cin[:, :, 0:HALO], 0.0)
            nc.gpsimd.memset(cin[:, :, HALO + L:CW], 0.0).then_inc(consts, 1)
            nc.gpsimd.memset(bq, 0.0).then_inc(bq_zero, 1)
            pool.wait_ge(etab, 1)

            def table(q):
                if q >= 2:
                    pool.wait_ge(tab_used, q - 1)
                ct, st = cosT[q % 2], sinT[q % 2]

                def e1(t):
                    return t[:, q * QB:(q + 1) * QB, 0:17].unsqueeze(3).to_broadcast([P, QB, 17, 16])

                def e2(t):
                    return t[:, q * QB:(q + 1) * QB, 17:33].unsqueeze(2).to_broadcast([P, QB, 17, 16])

                def grid(t):
                    return t.rearrange("p j (a b) -> p j a b", b=16)

                nc.gpsimd.tensor_tensor(grid(ct), e1(ec), e2(ec), ALU.mult)
                link(nc.gpsimd.tensor_tensor(grid(tabtmp), e1(es), e2(es), ALU.mult))
                link(nc.gpsimd.tensor_tensor(grid(ct), grid(ct), grid(tabtmp), ALU.subtract))
                nc.gpsimd.tensor_tensor(grid(st), e1(es), e2(ec), ALU.mult)
                link(nc.gpsimd.tensor_tensor(grid(tabtmp), e1(ec), e2(es), ALU.mult))
                link(nc.gpsimd.tensor_tensor(grid(st), grid(st), grid(tabtmp), ALU.add))
                nc.gpsimd.engine_nop().then_inc(tables, 1)

            def tap_matrices(m):
                nc.gpsimd.tensor_tensor(wtap, sel32[:, :].unsqueeze(1).unsqueeze(1).to_broadcast([P, TG, MT, 32]),
                                        cw[:, :, MT * m:MT * m + MT].unsqueeze(3).to_broadcast([P, TG, MT, 32]),
                                        ALU.mult).then_inc(taps_ready, 1)

            table(0)
            table(1)
            pool.wait_ge(cw_ready, 1)
            tap_matrices(0)
            pool.wait_ge(mm_act, 12)
            nc.gpsimd.tensor_tensor(cin[:, :, HALO:HALO + L], cin[:, :, HALO:HALO + L], cgate, ALU.mult
                                    ).then_inc(glu, 1)
            table(2)
            for m in (1, 2, 3):
                if m == 2:
                    table(3)
                pool.wait_ge(conv_mm, m)
                tap_matrices(m)
            pool.wait_ge(bgu_in, 16 * 3)
            link(nc.gpsimd.tensor_copy(bp, bgu))
            link(nc.gpsimd.tensor_tensor(bgu, bgu, bp, ALU.subtract))
            link(nc.gpsimd.tensor_copy(bg2, bgu))
            link(nc.gpsimd.tensor_tensor(bgu, bgu, bg2, ALU.subtract))
            link(nc.gpsimd.tensor_copy(bp[32:64, :], bg2[32:64, :]))
            link(nc.gpsimd.tensor_copy(bp[64:96, :], bgu[64:96, :]))
            nc.gpsimd.engine_nop().then_inc(bias_parts, 1)
            pool.wait_ge(shifts, 16 * MT * SH)
            link(nc.gpsimd.memset(upper, 1.0))
            nc.gpsimd.affine_select(out=upper, in_=upper, compare_op=ALU.is_gt, fill=0.0, base=0,
                                    pattern=[[1, P]], channel_multiplier=-1).then_inc(late_consts, 1)
            nc.gpsimd.memset(onesb, 1.0).then_inc(late_consts, 1)
            nc.gpsimd.iota(slots, pattern=[[0, 2], [1, BS]], base=0, channel_multiplier=0,
                           allow_small_or_imprecise_dtypes=True).then_inc(late_consts, 1)
            nc.gpsimd.iota(blks, pattern=[[1, NBC]], base=0, channel_multiplier=0,
                           allow_small_or_imprecise_dtypes=True).then_inc(late_consts, 1)
            link(nc.gpsimd.memset(tri, 1.0))
            nc.gpsimd.affine_select(out=tri, in_=tri, compare_op=ALU.is_ge, fill=0.0, base=0,
                                    pattern=[[1, EXP]], channel_multiplier=-1).then_inc(late_consts, 1)
            pool.wait_ge(ln_ready, 1)
            nc.gpsimd.memset(ebias, 0.0).then_inc(late_consts, 1)
            nc.gpsimd.memset(selT, 0.0).then_inc(late_consts, 1)
            nc.gpsimd.memset(ysb, 0.0).then_inc(y_ready, 1)
            for c in range(ST):
                pool.wait_ge(part1, c + 1)
                nc.gpsimd.tensor_tensor(hr[:, c, :], hf[:, c, :], hp[:, 0, c, :], ALU.subtract).then_inc(rest1, 1)
                pool.wait_ge(part2, c + 1)
                nc.gpsimd.tensor_tensor(hp[:, 2, c, :], hr[:, c, :], hp[:, 1, c, :], ALU.subtract).then_inc(parts, 1)

            for c in range(ST):
                pool.wait_ge(final_sum, c + 1)
                nc.gpsimd.tensor_tensor(hr[:, c, :], h2[:, c, :], gfin, ALU.mult).then_inc(times_g, 1)

        @block.scalar
        def _(act):
            n = [0]

            def link(ins):
                n[0] += 1
                ins.then_inc(act_step, 1)
                act.wait_ge(act_step, n[0])

            act.wait_ge(dve_step, 1)
            link(nc.scalar.activation(ss[:, 15:16], ss[:, 14:15], ACT.Sqrt))
            for c in range(3):
                rows = P if c < 2 else META
                act.wait_ge(x_in[c], 16)
                ins = nc.scalar.activation(junk[0:rows, :], xin[0:rows, c, :], ACT.Square,
                                           accum_out=ss[0:rows, c:c + 1])
                if c < 2:
                    link(ins)
            ins.then_inc(sumsq, 1)
            act.wait_ge(ms_ready, 1)
            nc.scalar.activation(ss[:, 9:12], ss[:, 6:9], ACT.Sqrt).then_inc(root, 1)
            act.wait_ge(scales, 1)
            nc.scalar.activation(xin[:, 1, :], xin[:, 1, :], ACT.Copy, scale=ss[:, 13:14]).then_inc(normed, 1)
            act.wait_ge(par_cols, 1)
            for k in range(1, KT, 2):
                act.wait_ge(h_tr, k + 1)
                nc.scalar.activation(hT[:, k, :], ps[:, k % 4, 0:L], ACT.Copy, scale=colp[:, k:k + 1]).then_inc(h_act, 1)
            def empty_z(z):
                act.wait_ge(mm, z + 1)
                b = z % 4
                if z < 4:
                    ins = nc.scalar.copy(uT[:, z, :], ps[:, b, 0:L])
                elif z < 12:
                    m = 2 * ((z - 4) // 4) + z % 2
                    if (z - 4) % 4 < 2:
                        ins = nc.scalar.copy(cin[:, m, HALO:HALO + L], ps[:, b, 0:L])
                    else:
                        ins = nc.scalar.activation(cgate[:, m, :], ps[:, b, 0:L], ACT.Sigmoid)
                else:
                    ins = nc.scalar.activation(gates[:, z - 12, :], ps[:, b, 0:S], ACT.Sigmoid)
                ins.then_inc(mm_act, 1)

            def empty_drive(q):
                if q == 0:
                    act.wait_ge(bc_tr, 16)
                if q:
                    act.wait_ge(drive_used, q)
                for n in range(8):
                    act.wait_ge(drive_mm, 8 * q + n + 1)
                    nc.scalar.copy(drive[:, n % 2, n // 2, :], ps[:, 4 + n % 2, 0:L]).then_inc(drive_sb, 1)

            def gelu(q):
                act.wait_ge(y_pre, q + 1)
                nc.scalar.activation(ya[:, q, :], ya[:, q, :], ACT.Gelu).then_inc(ya_ready, 1)

            for z in range(4):
                empty_z(z)
            act.wait_ge(phases, 1)
            nc.scalar.activation(es[:, :, :], phase, ACT.Sin).then_inc(sines, 1)
            nc.scalar.activation(ec[:, :, :], phase, ACT.Sin, scale=0.5).then_inc(sines, 1)
            for z in range(4, 7):
                empty_z(z)
            empty_z(7)
            act.wait_ge(bc_tr, 16)
            nc.scalar.copy(bT[:, :, :, :], ps[:, 4:6, :].rearrange("p a (m c) -> p a m c", c=P)).then_inc(bc_cols, 1)
            nc.scalar.copy(cT[:, :, :, :], ps[:, 6:8, :].rearrange("p a (m c) -> p a m c", c=P)).then_inc(bc_cols, 1)
            for step, m in PE_ORDER:
                if step == "z":
                    empty_z(m)
                elif step == "drives":
                    empty_drive(m)
                elif step == "conv":
                    act.wait_ge(conv_mm, m + 1)
                    if m == 0:
                        act.wait_ge(glu, 1)
                    nc.scalar.activation(cacc[:, m, :], ps[:, 7, (m % 2) * S:(m % 2) * S + S], ACT.Identity,
                                         bias=colp[:, 12 + m:13 + m]).then_inc(conv_sb, 1)
                elif step == "gelu":
                    act.wait_ge(centred, 1)
                    nc.scalar.activation(csq, cacc, ACT.Square).then_inc(squared, 1)
                    for q in range(MT):
                        gelu(q)

            def s5_gate(k):
                act.wait_ge(mm, S5_USE + k + 1)
                if k >= 2:
                    act.wait_ge(merge_ready, k - 1)
                nc.scalar.activation(sig[:, k % 2, :], ps[:, (S5_USE + k) % 4, S:2 * S], ACT.Sigmoid
                                     ).then_inc(gated, 1)

            act.wait_ge(var_ready, 1)
            nc.scalar.activation(lnr, lnv, ACT.Sqrt).then_inc(ln_root, 1)
            act.wait_ge(ln_ready, 1)
            for m in range(MT):
                nc.scalar.activation(cacc[:, m, :], cacc[:, m, :], ACT.Silu, scale=colp[:, 16 + m:17 + m],
                                     bias=colp[:, 20 + m:21 + m]).then_inc(conv_act, 1)
            for k in range(4):
                s5_gate(k)
            for k in range(4, KT):
                s5_gate(k)
            act.wait_ge(bias_parts, 1)
            link(nc.scalar.activation(ss[:, 15:16], ss[:, 14:15], ACT.Sqrt))
            for c in range(ST):
                act.wait_ge(h2_tr, 2 * c + 1)
                nc.scalar.copy(h2T[:, 0:4, c * P:(c + 1) * P], ps[:, 2 * c, :].rearrange("p (k t) -> p k t", t=P)
                               ).then_inc(h2T_act, 1)
                act.wait_ge(h2_ready, 2 * c + 2)
                nc.scalar.activation(hr[:, c, :], h2[:, c, :], ACT.Square, accum_out=ss[:, c:c + 1]).then_inc(sumsq, 1)
                act.wait_ge(ms_ready, 2 + c)
                nc.scalar.activation(ss[:, 9 + c:10 + c], ss[:, 6 + c:7 + c], ACT.Sqrt).then_inc(root, 1)
                act.wait_ge(hf_ready, c + 1)
                nc.scalar.copy(hp[:, 0, c, :], hf[:, c, :]).then_inc(part1, 1)
                act.wait_ge(top1, c + 1)
                nc.scalar.activation(ex[:, c, :], lg[:, c, :], ACT.Exp, bias=rs1[:, c:c + 1]).then_inc(exps, 1)
                act.wait_ge(rest1, c + 1)
                nc.scalar.copy(hp[:, 1, c, :], hr[:, c, :]).then_inc(part2, 1)
                if c == 0:
                    link(nc.scalar.activation(ss[:, 15:16], ss[:, 14:15], ACT.Sqrt))

            act.wait_ge(gather_mm, 1)
            nc.scalar.copy(xT, ps[:, 3, :].rearrange("p (k s) -> p k s", s=BS)).then_inc(xT_ready, 1)
            act.wait_ge(plan, 1)
            total = act.value_load(blk_until[0:1, EXP - 1:EXP], min_val=EXP, max_val=NBLK)

            def one_block(i):
                act.wait_ge(g1_ready, i + 1)
                nc.scalar.activation(sg, g1, ACT.Sigmoid, scale=ALPHA).then_inc(sg_ready, 1)
                act.wait_ge(act_tr, i + 1)
                nc.scalar.copy(actT, ps[:, 0, :].rearrange("p (j s) -> p j s", s=P)).then_inc(actT_ready, 1)
                act.wait_ge(gather_mm, i + 2)
                nc.scalar.copy(xT, ps[:, 3, :].rearrange("p (k s) -> p k s", s=BS)).then_inc(xT_ready, 1)
                act.wait_ge(dn_done, i * KT + KT)
                nc.scalar.copy(ysb, ps[:, 2, :]).then_inc(y_ready, 1)

            with act.Fori(0, EXP) as i:
                one_block(i)
            with act.Fori(0, (NBLK - EXP) // TURNS) as turn:
                with act.If(EXP + turn * TURNS < total):
                    with act.Fori(0, TURNS) as t:
                        with act.If(EXP + turn * TURNS + t < total):
                            one_block(EXP + turn * TURNS + t)
            for c in range(ST):
                act.wait_ge(final_sum, c + 1)
                nc.scalar.activation(hf[:, c, :], h2[:, c, :], ACT.Square, accum_out=ss[:, c:c + 1]).then_inc(sumsq, 1)
                act.wait_ge(ms_ready, 4 + c)
                nc.scalar.activation(ss[:, 9 + c:10 + c], ss[:, 6 + c:7 + c], ACT.Sqrt).then_inc(root, 1)

        @block.vector
        def _(dve):
            n = [0]

            def link(ins):
                n[0] += 1
                ins.then_inc(dve_step, 1)
                dve.wait_ge(dve_step, n[0])

            def rsqrt(at, width):
                a, r, o, t = (ss[:, k + at:k + at + width] for k in (6, 9, 12, 9))
                link(nc.vector.reciprocal(o, r))
                link(nc.vector.tensor_tensor(t, a, o, ALU.mult))
                link(nc.vector.tensor_tensor(t, t, o, ALU.mult))
                link(nc.vector.tensor_scalar(t, t, -0.5, 1.5, ALU.mult, ALU.add))
                link(nc.vector.tensor_tensor(o, o, t, ALU.mult))

            def exp(o, x, w, rows):
                y, k, r, p = (xs[0:rows, c, 0:w] for c in range(4))
                ki = xi[0:rows, 0:w]
                link(nc.vector.tensor_scalar(y, x, -88.0, 88.0, ALU.max, ALU.min))
                link(nc.vector.tensor_scalar(k, y, 1.4426950408889634, MAGIC, ALU.mult, ALU.add))
                link(nc.vector.tensor_scalar(k, k, -MAGIC, None, ALU.add))
                link(nc.vector.scalar_tensor_tensor(r, k, -LN2[0], y, ALU.mult, ALU.add))
                link(nc.vector.scalar_tensor_tensor(r, k, -LN2[1], r, ALU.mult, ALU.add))
                fact = [1.0]
                for c in range(1, 9):
                    fact.append(fact[-1] / c)
                link(nc.vector.tensor_scalar(p, r, fact[8], None, ALU.mult))
                for c in range(7, 0, -1):
                    link(nc.vector.scalar_tensor_tensor(p, p, fact[c], r, ALU.add, ALU.mult))
                link(nc.vector.tensor_scalar(p, p, 1.0, None, ALU.add))
                link(nc.vector.tensor_scalar(ki, k, 127.0, None, ALU.add))
                link(nc.vector.tensor_scalar(ki, ki, 23, None, ALU.logical_shift_left))
                link(nc.vector.tensor_tensor(o, p, ki.bitcast(F32), ALU.mult))

            def wrap(x, k):
                link(nc.vector.tensor_scalar(k, x, 1.0 / (2 * np.pi), MAGIC, ALU.mult, ALU.add))
                link(nc.vector.tensor_scalar(k, k, -MAGIC, None, ALU.add))
                for c in TWO_PI:
                    link(nc.vector.scalar_tensor_tensor(x, k, -c, x, ALU.mult, ALU.add))
                link(nc.vector.tensor_scalar(x, x, -3.1415925, 3.1415925, ALU.max, ALU.min))

            link(nc.vector.memset(ss[:, :], 1.0))
            dve.wait_ge(consts, 7)
            link(nc.vector.tensor_reduce(hmask[:, :], seg[:, :].rearrange("p (j h) -> p h j", h=2), AX_X, ALU.add))
            link(nc.vector.tensor_reduce(jmask[:, :], seg[:, :].rearrange("p (j h) -> p j h", h=2), AX_X, ALU.add))
            link(nc.vector.tensor_copy(pmod[:, :], pidx[:, :]))
            for j in range(1, 4):
                link(nc.vector.scalar_tensor_tensor(pmod[:, :], jmask[:, j:j + 1], -32.0 * j, pmod[:, :], ALU.mult,
                                                    ALU.add))
            link(nc.vector.tensor_reduce(sel32[:, :], ident[:, :].rearrange("p (h c) -> p c h", c=32), AX_X, ALU.add))
            dve.wait_ge(sumsq, 1)
            link(nc.vector.tensor_scalar(ss[:, 6:9], ss[:, 0:3], 1.0 / D, EPS_RMS, ALU.mult, ALU.add))
            nc.vector.engine_nop().then_inc(ms_ready, 1)
            dve.wait_ge(root, 1)
            rsqrt(0, 3)
            nc.vector.engine_nop().then_inc(scales, 1)
            for c, rows in ((0, P), (2, META)):
                nc.vector.tensor_scalar(xin[0:rows, c, :], xin[0:rows, c, :], ss[0:rows, 12 + c:13 + c], None,
                                        ALU.mult).then_inc(normed, 1)
            dve.wait_ge(par_tr, 1)
            nc.vector.tensor_copy(colp[:, :], ps[:, 7, 0:32]).then_inc(par_cols, 1)
            dve.wait_ge(par_cols, 1)
            for k in range(0, KT, 2):
                dve.wait_ge(h_tr, k + 1)
                nc.vector.tensor_scalar(hT[:, k, :], ps[:, k % 4, 0:L], colp[:, k:k + 1], None, ALU.mult
                                        ).then_inc(h_dve, 1)
            dve.wait_ge(par_in, 16 * 3)
            exp(dts, ldt, 2, NB)
            for c in range(2):
                ins = nc.vector.tensor_tensor(arow[:, c, :].rearrange("b (g p) -> b g p", g=2),
                                              arow[:, 2 + c, :].rearrange("b (g p) -> b g p", g=2),
                                              dts.unsqueeze(2).to_broadcast([NB, 2, 64]), ALU.mult)
            ins.then_inc(disc_rows, 1)
            dve.wait_ge(disc_tr, 1)
            link(nc.vector.tensor_copy(pc[:, :, :], ps[:, 6, 0:4 * NB].rearrange("p (a b) -> p a b", b=NB)))
            exp(decay, pc[:, 0, :], NB, P)
            th = pc[:, 1, :]
            t16, kk = xs[:, 4, :], xs[:, 5, :]
            wrap(th, kk)
            link(nc.vector.tensor_scalar(t16, th, 16.0, None, ALU.mult))
            wrap(t16, kk)
            link(nc.vector.tensor_tensor(phase[:, :, 0:17], t16.unsqueeze(2).to_broadcast([P, NB, 17]),
                                         expo[:, :].unsqueeze(1).to_broadcast([P, NB, 17]), ALU.mult))
            link(nc.vector.tensor_tensor(phase[:, :, 17:33], th.unsqueeze(2).to_broadcast([P, NB, 16]),
                                         expo[:, 0:16].unsqueeze(1).to_broadcast([P, NB, 16]), ALU.mult))
            wrap(phase, es[:, :, :])
            nc.vector.engine_nop().then_inc(phases, 1)
            dve.wait_ge(sines, 2)
            link(nc.vector.tensor_tensor(ec[:, :, :], ec[:, :, :], ec[:, :, :], ALU.mult))
            nc.vector.tensor_scalar(ec[:, :, :], ec[:, :, :], -2.0, 1.0, ALU.mult, ALU.add).then_inc(etab, 1)
            dve.wait_ge(etab, 1)
            are, aim = pc[:, 2, :], pc[:, 3, :]
            t0, t1 = xs[:, 0, :], xs[:, 1, :]
            TT = nc.vector.tensor_tensor
            link(TT(abr, decay, ec[:, :, 18], ALU.mult))
            link(TT(abi, decay, es[:, :, 18], ALU.mult))
            link(nc.vector.tensor_scalar(abr, abr, -1.0, None, ALU.add))
            link(TT(den, are, are, ALU.mult))
            link(TT(t0, aim, aim, ALU.mult))
            link(TT(den, den, t0, ALU.add))
            link(nc.vector.reciprocal(t0, den))
            link(TT(cre, abr, are, ALU.mult))
            link(TT(t1, abi, aim, ALU.mult))
            link(TT(cre, cre, t1, ALU.add))
            link(TT(cre, cre, t0, ALU.mult))
            link(TT(cim, abi, are, ALU.mult))
            link(TT(t1, abr, aim, ALU.mult))
            link(TT(cim, cim, t1, ALU.subtract))
            link(TT(cim, cim, t0, ALU.mult))
            dve.wait_ge(bq_zero, 1)
            dve.wait_ge(bc_in, 16 * 4)
            crb = cre.unsqueeze(2).to_broadcast([P, NB, 16])
            cib = cim.unsqueeze(2).to_broadcast([P, NB, 16])
            for ri, op in ((0, ALU.subtract), (1, ALU.add)):
                link(TT(pt1, crb, bn[:, ri, :, :], ALU.mult))
                link(TT(pt2, cib, bn[:, 1 - ri, :, :], ALU.mult))
                for g in range(2):
                    link(TT(bq[64 * g:64 * g + 64, ri, :, g, :], pt1[64 * g:64 * g + 64], pt2[64 * g:64 * g + 64], op))
            for g in range(2):
                for ri, sign in ((0, 1.0), (1, -1.0)):
                    link(nc.vector.tensor_scalar(cq[:, ri, :, g, :], cn[:, ri, :, :], hmask[:, g:g + 1], sign,
                                                 ALU.mult, ALU.mult))
            nc.vector.engine_nop().then_inc(bc_ready, 1)
            dve.wait_ge(par_tr, 2)
            link(nc.vector.tensor_copy(cw[:, :, :], ps[:, 5, 0:P].rearrange("p (a q) -> p a q", a=TG)))
            nc.vector.memset(cw[96:128, TG - 1, :], 0.0).then_inc(cw_ready, 1)

            dve.wait_ge(bc_cols, 2)

            def spread_b(q):
                if q:
                    dve.wait_ge(drive_mm, 8 * q)
                for ri in range(2):
                    ins = TT(bz[:, ri, :, :], bT[:, ri, q:q + 1, :].to_broadcast([P, QB, P]),
                             jmask[:, :].unsqueeze(2).to_broadcast([P, QB, P]), ALU.mult)
                ins.then_inc(bz_ready, 1)

            def ypre(q):
                dve.wait_ge(y_mm, q + 1)
                nc.vector.scalar_tensor_tensor(ya[:, q, :], uT[:, q, META:], colp[:, 8 + q:9 + q], ps[:, 6, 0:S],
                                               ALU.mult, ALU.add).then_inc(y_pre, 1)

            spread_b(0)
            for q in range(MT):
                dve.wait_ge(drive_sb, 8 * (q + 1))
                dve.wait_ge(tables, q + 1)
                ct, st = cosT[q % 2], sinT[q % 2]
                if q + 1 < MT:
                    spread_b(q + 1)
                TT(rot[:, 0, :, :], drive[:, 0, :, :], ct, ALU.mult)
                link(TT(rtmp, drive[:, 1, :, :], st, ALU.mult))
                link(TT(rot[:, 0, :, :], rot[:, 0, :, :], rtmp, ALU.add))
                TT(rot[:, 1, :, :], drive[:, 1, :, :], ct, ALU.mult)
                link(TT(rtmp, drive[:, 0, :, :], st, ALU.mult))
                nc.vector.engine_nop().then_inc(drive_used, 1)
                link(TT(rot[:, 1, :, :], rot[:, 1, :, :], rtmp, ALU.subtract))
                for j in range(QB):
                    for ri in range(2):
                        ins = nc.vector.tensor_tensor_scan(
                            rot[:, ri, j, :], decay[:, q * QB + j:q * QB + j + 1].to_broadcast([P, L]),
                            rot[:, ri, j, :], 0.0, ALU.mult, ALU.add)
                link(ins)
                wr, wi = rot[:, 0, :, META:], rot[:, 1, :, META:]
                cs, sn, tm = ct[:, :, META:], st[:, :, META:], rtmp[:, :, META:]
                pr, pi = prod[:, q % 2, 0, :, :], prod[:, q % 2, 1, :, :]
                if q == 0:
                    dve.wait_ge(h_tr, KT)
                elif q >= 2:
                    dve.wait_ge(y_mm, q - 1)
                TT(pr, wr, cs, ALU.mult)
                link(TT(tm, wi, sn, ALU.mult))
                link(TT(pr, pr, tm, ALU.subtract))
                TT(pi, wr, sn, ALU.mult)
                link(TT(tm, wi, cs, ALU.mult))
                link(TT(pi, pi, tm, ALU.add))
                nc.vector.engine_nop().then_inc(states, 1)
                nc.vector.engine_nop().then_inc(tab_used, 1)
                if q:
                    ypre(q - 1)

            ypre(MT - 1)
            dve.wait_ge(mean_mm, 1)
            nc.vector.tensor_tensor(cacc, cacc, ps[:, 7:8, 0:S].to_broadcast([P, MT, S]), ALU.subtract
                                    ).then_inc(centred, 1)
            dve.wait_ge(var_mm, 1)
            nc.vector.tensor_scalar(lnv, ps[:, 7, S:2 * S], EPS_LN, None, ALU.add).then_inc(var_ready, 1)
            dve.wait_ge(ln_root, 1)
            link(nc.vector.reciprocal(lnt, lnr))
            link(TT(lnr, lnv, lnt, ALU.mult))
            link(TT(lnr, lnr, lnt, ALU.mult))
            link(nc.vector.tensor_scalar(lnr, lnr, -0.5, 1.5, ALU.mult, ALU.add))
            link(TT(lnt, lnt, lnr, ALU.mult))
            TT(cacc, cacc, lnt.unsqueeze(1).to_broadcast([P, MT, S]), ALU.mult).then_inc(ln_ready, 1)

            def s5_merge(n):
                use = S5_USE + n
                dve.wait_ge(gated, n + 1)
                dve.wait_ge(mm, use + 1)
                link(TT(mtmp[:, 0, :], ps[:, use % 4, 0:S], sig[:, n % 2, :], ALU.mult))
                nc.vector.engine_nop().then_inc(mm_dve, 1)
                TT(merged[:, n, :], mtmp[:, 0, :], gates[:, n, :], ALU.mult).then_inc(merge_ready, 1)
                dve.wait_ge(merge_ready, n + 1)

            for n_ in range(KT):
                s5_merge(n_)
            for m in range(KT):
                use = CO_USE + m
                dve.wait_ge(mm, use + 1)
                link(TT(mtmp[:, 1, :], ps[:, use % 4, 0:S], gates[:, KT + m, :], ALU.mult))
                nc.vector.engine_nop().then_inc(mm_dve, 1)
                TT(merged[:, m, :], merged[:, m, :], mtmp[:, 1, :], ALU.add).then_inc(merge_ready, 1)
                dve.wait_ge(merge_ready, KT + m + 1)
            dve.wait_ge(rw_in, 32)
            TT(rw, rw, colp[:, 24:32].unsqueeze(2).to_broadcast([P, KT, EXP]), ALU.mult).then_inc(rw_ready, 1)
            dve.wait_ge(xres_in, 32)
            dve.wait_ge(late_in, 32)
            dve.wait_ge(bias_parts, 1)
            dve.wait_ge(late_consts, 7)

            def second_norm(c):
                for h in range(2):
                    dve.wait_ge(wo_mm, 2 * c + h + 1)
                    part = h2[:, c, 512 * h:512 * h + 512]
                    TT(part, part, ps[:, 4 + 2 * c + h, :], ALU.add).then_inc(h2_ready, 1)
                dve.wait_ge(h2_ready, 2 * c + 2)
                dve.wait_ge(h2_tr, 2 * c + 2)
                nc.vector.tensor_copy(h2T[:, 4:8, c * P:(c + 1) * P], ps[:, 2 * c + 1, :].rearrange(
                    "p (k t) -> p k t", t=P)).then_inc(h2T_dve, 1)
                dve.wait_ge(sumsq, 2 + c)
                nc.vector.tensor_scalar(ss[:, 6 + c:7 + c], ss[:, c:c + 1], 1.0 / D, EPS_RMS, ALU.mult, ALU.add
                                        ).then_inc(ms_ready, 1)
                dve.wait_ge(root, 2 + c)
                rsqrt(c, 1)
                nc.vector.scalar_tensor_tensor(hf[:, c, :], h2[:, c, :], ss[:, 12 + c:13 + c], gffn, ALU.mult,
                                               ALU.mult).then_inc(hf_ready, 1)

            def choose(c):
                dve.wait_ge(logit_mm, c + 1)
                link(nc.vector.scalar_tensor_tensor(lg[:, c, :], ps[:, 2 * c, 0:EXP], ss[:, 12 + c:13 + c], rb,
                                                    ALU.mult, ALU.add))
                link(nc.vector.max(v8[:, c, :], lg[:, c, :]))
                nc.vector.tensor_scalar(rs1[:, c:c + 1], v8[:, c, 0:1], -1.0, None, ALU.mult).then_inc(top1, 1)
                v4 = v8[:, c, TOPK - 1:TOPK].to_broadcast([P, EXP])
                TT(eq[:, c, :], lg[:, c, :], v4, ALU.is_equal)
                link(TT(gt[:, c, :], lg[:, c, :], v4, ALU.is_gt))
                nc.vector.tensor_reduce(rs1[:, 2 + c:3 + c], gt[:, c, :], AX_X, ALU.add)
                link(nc.vector.tensor_tensor_scan(ce[:, c, :], ones[:, 0:EXP], eq[:, c, :], 0.0, ALU.mult, ALU.add))
                link(nc.vector.tensor_scalar(rs1[:, 4 + c:5 + c], rs1[:, 2 + c:3 + c], -1.0, float(TOPK), ALU.mult,
                                             ALU.add))
                link(nc.vector.scalar_tensor_tensor(ce[:, c, :], ce[:, c, :], rs1[:, 4 + c:5 + c], eq[:, c, :],
                                                    ALU.is_le, ALU.mult))
                link(TT(mask[:, c, :], gt[:, c, :], ce[:, c, :], ALU.add))
                nc.vector.tensor_copy(maskb[:, c, :], mask[:, c, :]).then_inc(masks, 1)
                link(nc.vector.tensor_scalar(posm[:, c, :], mask[:, c, :], -BIG, BIG, ALU.mult, ALU.add))

            def weigh(c):
                dve.wait_ge(exps, c + 1)
                link(TT(ex[:, c, :], ex[:, c, :], mask[:, c, :], ALU.mult))
                link(nc.vector.tensor_reduce(rs1[:, 6 + c:7 + c], ex[:, c, :], AX_X, ALU.add))
                link(nc.vector.reciprocal(rs1[:, 8 + c:9 + c], rs1[:, 6 + c:7 + c]))
                link(nc.vector.tensor_scalar(comb[:, c, :], ex[:, c, :], rs1[:, 8 + c:9 + c], None, ALU.mult))

            second_norm(0)
            choose(0)
            weigh(0)
            second_norm(1)
            choose(1)

            def ebias_for(i):
                for h in range(2):
                    ins = nc.vector.tensor_copy(ebias[:, h, BS * h:BS * h + BS],
                                                bk[:, bass.ds(i, 1)].to_broadcast([P, BS]))
                return ins

            def onehot_for():
                for c in range(ST):
                    ins = nc.vector.tensor_scalar(onehot[:, c, :], slots[:, 0, :], cur[:, c:c + 1], None, ALU.is_equal)
                return ins

            dve.wait_ge(count_mm, 1)
            cnt, nb = ps[0:EXP, 3, 0:1], rs1[0:EXP, 11:12]
            link(nc.vector.tensor_scalar(nb, cnt, float(BS), 1.0, ALU.is_gt, ALU.add))
            for b in range(2, S // BS):
                link(nc.vector.scalar_tensor_tensor(nb, cnt, float(BS * b), nb, ALU.is_gt, ALU.add))
            nc.vector.engine_nop().then_inc(blocks_ready, 1)
            link(TT(posm, posm, ps[:, 1, 0:ST * EXP].rearrange("p (c e) -> p c e", e=EXP), ALU.add))
            nc.vector.tensor_copy(cur[:, 0:2], posm[:, :, 0])
            link(nc.vector.tensor_scalar(bk[:, 0:1], pmod[:, :], 0.0, None, ALU.is_equal))
            ebias_for(0)
            onehot_for().then_inc(onehot_ready, 1)
            dve.wait_ge(plan_tr, 1)
            link(nc.vector.tensor_copy(rs1[0:EXP, 12:13], ps[0:EXP, 2, 32:33]))
            nc.vector.tensor_scalar(nbb, ones[0:EXP, :], nb, None, ALU.mult)
            link(nc.vector.tensor_scalar(cmp, blks[0:EXP, :], rs1[0:EXP, 12:13], None, ALU.is_ge))
            nc.vector.engine_nop().then_inc(plan_cols, 1)
            nc.vector.tensor_copy(blk_until[:, :], ps[0:1, 2, 64:64 + EXP])
            nc.vector.tensor_scalar(blk_last[:, :], ps[0:1, 2, 64:64 + EXP], -1.0, None, ALU.add)
            dve.wait_ge(plan_mm, 1)
            link(nc.vector.tensor_copy(blk_expert[:, :], ps[0:1, 1, 128:128 + NBC]))
            link(nc.vector.tensor_scalar(blk_odd[:, :], blk_expert[:, :], 1, None, ALU.bitwise_and))
            nc.vector.engine_nop().then_inc(plan, 1)
            link(nc.vector.tensor_scalar(bk, ps[:, 1, 128:128 + NBC], pmod[:, :], None, ALU.is_equal))
            link(TT(off, blks, ps[:, 1, 192:192 + NBC], ALU.subtract))
            link(nc.vector.tensor_scalar(off, off, float(BS), None, ALU.mult))
            weigh(1)
            nc.vector.engine_nop().then_inc(pos_ready, 1)
            nc.vector.tensor_copy(cur[:, 2:4], comb[:, :, 0])
            dve.wait_ge(pc_tr, 1)
            link(nc.vector.tensor_copy(pcT, ps[0:EXP, 2, :].rearrange("p (a t) -> p a t", t=P)))
            nc.vector.tensor_copy(selT[0:EXP, 0, :], ps[0:EXP, 2, S:2 * S])
            nc.vector.tensor_copy(selT[64:64 + EXP, 1, :], ps[0:EXP, 2, S:2 * S]).then_inc(selT_ready, 1)
            dve.wait_ge(plan_sel, 1)
            sel = ps[:, 2, 0:4 * NBC].rearrange("p (a b) -> p a b", b=NBC)
            link(TT(blkcol[:, 0:2, :], sel[:, 0:2, :], off.unsqueeze(1).to_broadcast([P, 2, NBC]), ALU.subtract))
            link(nc.vector.tensor_copy(blkcol[:, 2:4, :], sel[:, 2:4, :]))
            nc.vector.engine_nop().then_inc(blk_step, 1)
            total = dve.value_load(blk_until[0:1, EXP - 1:EXP], min_val=EXP, max_val=NBLK)

            def one_block(i):
                dve.wait_ge(onehot_ready, i + 1)
                for c in range(ST):
                    ins = nc.vector.tensor_scalar(wsel[:, c, :], slots.rearrange("p a b -> p (a b)"), cur[:, c:c + 1],
                                                  cur[:, 2 + c:3 + c], ALU.is_equal, ALU.mult)
                ins.then_inc(wsel_ready, 1)
                dve.wait_ge(wsel_ready, i + 1)
                nc.vector.tensor_copy(cur, blkcol[:, :, bass.ds(i + 1, 1)].rearrange("p a b -> p (a b)")
                                      ).then_inc(blk_step, 1)
                dve.wait_ge(blk_step, i + 2)
                dve.wait_ge(gather_mm, i + 1)
                dve.wait_ge(gu_done, i * KT + 1)
                ebias_for(i + 1)
                onehot_for().then_inc(onehot_ready, 1)
                dve.wait_ge(gu_done, i * KT + KT)
                nc.vector.tensor_scalar(g1, ps[:, 0, :], LIMIT, None, ALU.min).then_inc(g1_ready, 1)
                nc.vector.tensor_scalar(l1, ps[:, 1, :], LIMIT, -LIMIT, ALU.min, ALU.max).then_inc(l1_ready, 1)
                dve.wait_ge(g1_ready, i + 1)
                dve.wait_ge(l1_ready, i + 1)
                nc.vector.scalar_tensor_tensor(l1, l1, 1.0, g1, ALU.add, ALU.mult).then_inc(m_ready, 1)
                dve.wait_ge(m_ready, i + 1)
                dve.wait_ge(sg_ready, i + 1)
                nc.vector.tensor_tensor(l1, l1, sg, ALU.mult).then_inc(act_ready, 1)
                dve.wait_ge(sel_tr, i + 1)
                nc.vector.tensor_copy(selT[0:64, 0, :], ps[0:64, 1, 0:S])
                nc.vector.tensor_copy(selT[64:128, 1, :], ps[64:128, 1, 0:S]).then_inc(selT_ready, 1)

            with dve.Fori(0, EXP) as i:
                one_block(i)
            with dve.Fori(0, (NBLK - EXP) // TURNS) as turn:
                with dve.If(EXP + turn * TURNS < total):
                    with dve.Fori(0, TURNS) as t:
                        with dve.If(EXP + turn * TURNS + t < total):
                            one_block(EXP + turn * TURNS + t)
            for c in range(ST):
                for h in range(2):
                    dve.wait_ge(scattered, 2 * c + h + 1)
                    part = h2[:, c, 512 * h:512 * h + 512]
                    link(TT(part, part, ps[:, 4 + 2 * c + h, :], ALU.add))
                nc.vector.engine_nop().then_inc(final_sum, 1)
            for c in range(ST):
                dve.wait_ge(sumsq, 4 + c)
                nc.vector.tensor_scalar(ss[:, 6 + c:7 + c], ss[:, c:c + 1], 1.0 / D, EPS_RMS, ALU.mult, ALU.add
                                        ).then_inc(ms_ready, 1)
                dve.wait_ge(root, 4 + c)
                rsqrt(c, 1)
                dve.wait_ge(times_g, c + 1)
                nc.vector.tensor_scalar(h2[:, c, :], hr[:, c, :], ss[:, 12 + c:13 + c], None, ALU.mult
                                        ).then_inc(result, 1)

        @block.tensor
        def _(pe):
            pe.wait_ge(consts, 7)
            pe.wait_ge(rows_in, 16 * 6)
            nc.tensor.transpose(ps[:, 7, 0:32], rows1, ident[0:32, 0:32]).then_inc(par_tr, 1)
            pe.wait_ge(normed, 3)
            for k in range(KT):
                if k >= 4:
                    pe.wait_ge(h_dve if k % 2 == 0 else h_act, (k - 4) // 2 + 1)
                b = ps[:, k % 4, :]
                nc.tensor.transpose(b[:, 0:META], xin[0:META, 2, k * P:(k + 1) * P], ident[0:META, 0:META])
                nc.tensor.transpose(b[:, META:META + P], xin[:, 0, k * P:(k + 1) * P], ident[:, :])
                nc.tensor.transpose(b[:, META + P:L], xin[:, 1, k * P:(k + 1) * P], ident[:, :]).then_inc(h_tr, 1)
            pe.wait_ge(h_dve, 4)
            pe.wait_ge(h_act, 4)

            def z_tile(z):
                ld = z // 2
                if z % 2 == 0:
                    pe.wait_ge(slot_in[ld % MSLOT], 16 * (ld // MSLOT + 1))
                if z >= 4:
                    emptied(pe, z - 4)
                w = slot(ld, (KT, 256))
                n0 = 0 if z < 12 else META
                for k in range(KT):
                    ins = nc.tensor.matmul(ps[:, z % 4, 0:L - n0], w[:, k, (z % 2) * P:(z % 2) * P + P], hT[:, k, n0:L],
                                           start=(k == 0), stop=(k == KT - 1))
                ins.then_inc(mm, 1)

            def drives(q):
                pe.wait_ge(bz_ready, q + 1)
                for j in range(QB):
                    for ri in range(2):
                        n = 8 * q + 2 * j + ri
                        if n >= 2:
                            pe.wait_ge(drive_sb, n - 1)
                        else:
                            pe.wait_ge(bc_cols, 2)
                        nc.tensor.matmul(ps[:, 4 + ri, 0:L], bz[:, ri, j, :], uT[:, q, :], start=True, stop=True
                                         ).then_inc(drive_mm, 1)

            def outputs(q):
                pe.wait_ge(states, q + 1)
                if q:
                    pe.wait_ge(y_pre, q)
                for ri in range(2):
                    for j in range(QB):
                        ins = nc.tensor.matmul(ps[32 * j:32 * j + 32, 6, 0:S], cT[:, ri, q, 32 * j:32 * j + 32],
                                               prod[:, q % 2, ri, j, :], start=(ri == 0), stop=(ri == 1),
                                               tile_position=(0, 32 * j))
                ins.then_inc(y_mm, 1)

            def conv(m):
                pe.wait_ge(taps_ready, m + 1)
                if m == 0:
                    pe.wait_ge(shifts, 16 * MT * SH)
                if m:
                    pe.wait_ge(conv_sb, m)
                for a in range(TG):
                    for g in range(MT):
                        ins = nc.tensor.matmul(ps[32 * g:32 * g + 32, 7, (m % 2) * S:(m % 2) * S + S],
                                               wtap[:, a, g, :], shifted[:, m, g, SH * a:SH * a + S],
                                               start=(a == 0), stop=(a == TG - 1), tile_position=(0, 32 * g))
                ins.then_inc(conv_mm, 1)

            def mean():
                pe.wait_ge(conv_sb, MT)
                for m in range(MT):
                    ins = nc.tensor.matmul(ps[:, 7, 0:S], invc[:, :], cacc[:, m, :], start=(m == 0), stop=(m == MT - 1))
                ins.then_inc(mean_mm, 1)

            def variance():
                pe.wait_ge(squared, 1)
                for m in range(MT):
                    ins = nc.tensor.matmul(ps[:, 7, S:2 * S], invc[:, :], csq[:, m, :], start=(m == 0),
                                           stop=(m == MT - 1))
                ins.then_inc(var_mm, 1)

            for z in range(7):
                z_tile(z)
                if z == 0:
                    pe.wait_ge(disc_rows, 1)
                    for c in range(4):
                        ins = nc.tensor.transpose(ps[:, 6, NB * c:NB * c + NB], arow[:, c, :], ident[0:NB, 0:NB])
                    ins.then_inc(disc_tr, 1)
                if z == 3:
                    pe.wait_ge(tap_in, 16 * (TG + 1))
                    nc.tensor.transpose(ps[:, 5, 0:P], rows2, ident[:, :]).then_inc(par_tr, 1)
            z_tile(7)
            pe.wait_ge(bc_ready, 1)
            pe.wait_ge(cw_ready, 1)
            for ri in range(2):
                for q in range(MT):
                    nc.tensor.transpose(ps[:, 4 + ri, q * P:(q + 1) * P],
                                        bq[:, ri, q * QB:(q + 1) * QB, :, :].rearrange("p j g h -> p (j g h)"),
                                        ident[:, :]).then_inc(bc_tr, 1)
                    nc.tensor.transpose(ps[:, 6 + ri, q * P:(q + 1) * P],
                                        cq[:, ri, q, :, :].rearrange("p g s -> p (g s)"), ident[:, :]
                                        ).then_inc(bc_tr, 1)
            for step, n in PE_ORDER:
                if step == "z":
                    z_tile(n)
                elif step == "drives":
                    drives(n)
                elif step == "outputs":
                    outputs(n)
                elif step == "conv":
                    conv(n)
                elif step == "mean":
                    mean()
            variance()

            pe.wait_ge(ya_ready, MT)
            for n in range(KT):
                use = S5_USE + n
                emptied(pe, use - 4)
                for g in range(2):
                    ld = N_IN + 2 * (n // 4) + g
                    if n % 4 == 0:
                        pe.wait_ge(slot_in[ld % MSLOT], 16 * (ld // MSLOT + 1))
                    w = slot(ld, (MT, 512))
                    for k in range(MT):
                        ins = nc.tensor.matmul(ps[:, use % 4, g * S:(g + 1) * S], w[:, k, (n % 4) * P:(n % 4) * P + P],
                                               ya[:, k, :], start=(k == 0), stop=(k == MT - 1))
                ins.then_inc(mm, 1)
            pe.wait_ge(conv_act, MT)
            for n in range(KT):
                ld, use = N_IN + 4 + n // 4, CO_USE + n
                if n % 4 == 0:
                    pe.wait_ge(slot_in[ld % MSLOT], 16 * (ld // MSLOT + 1))
                emptied(pe, use - 4)
                w = slot(ld, (MT, 512))
                for k in range(MT):
                    ins = nc.tensor.matmul(ps[:, use % 4, 0:S], w[:, k, (n % 4) * P:(n % 4) * P + P], cacc[:, k, :],
                                           start=(k == 0), stop=(k == MT - 1))
                ins.then_inc(mm, 1)

            def residual_cols(c):
                for h in range(2):
                    pe.wait_ge(h2_ready, 2 * c + h + 1)
                    if c == 0:
                        pe.wait_ge(merge_ready, 2 * KT)
                    for k in range(4 * h, 4 * h + 4):
                        ins = nc.tensor.transpose(ps[:, 2 * c + h, (k % 4) * P:(k % 4) * P + P],
                                                  h2[:, c, k * P:(k + 1) * P], ident[:, :])
                    ins.then_inc(h2_tr, 1)

            def logits(c):
                pe.wait_ge(h2T_act, c + 1)
                pe.wait_ge(h2T_dve, c + 1)
                pe.wait_ge(rw_ready, 1)
                for k in range(KT):
                    ins = nc.tensor.matmul(ps[:, 2 * c, 0:EXP], h2T[:, k, c * P:(c + 1) * P], rw[:, k, :],
                                           start=(k == 0), stop=(k == KT - 1))
                ins.then_inc(logit_mm, 1)

            for c in range(ST):
                for k in range(KT):
                    ld = N_IN + 6 + k // 2
                    if c == 0:
                        pe.wait_ge(merge_ready, KT + k + 1)
                        if k % 2 == 0:
                            pe.wait_ge(slot_in[ld % MSLOT], 16 * (ld // MSLOT + 1))
                    w = slot(ld, (2, 1024))
                    for h in range(2):
                        ins = nc.tensor.matmul(ps[:, 4 + 2 * c + h, :], merged[:, k, c * P:(c + 1) * P],
                                               w[:, k % 2, 512 * h:512 * h + 512], start=(k == 0), stop=(k == KT - 1))
                        if k == KT - 1:
                            ins.then_inc(wo_mm, 1)
                    if c == 1:
                        if k % 2 and k < KT - 1:
                            ins.then_inc(wo_used, 1)
                        if k == 1:
                            residual_cols(0)
                        if k == 3:
                            logits(0)
            residual_cols(1)
            logits(1)
            pe.wait_ge(late_consts, 7)
            for b in range(4, 8):
                nc.tensor.matmul(ps[:, b, :], ebias[:, 0, :], upper.unsqueeze(1).to_broadcast([P, 4, P]), start=True,
                                 stop=False, skip_group_check=True)
            pe.wait_ge(masks, 2)
            nc.tensor.matmul(ps[:, 1, 0:EXP], upper, maskb[:, 0, :], start=True, stop=True)
            nc.tensor.matmul(ps[:, 1, EXP:2 * EXP], onesb, maskb[:, 0, :], start=True, stop=False)
            nc.tensor.matmul(ps[:, 1, EXP:2 * EXP], upper, maskb[:, 1, :], start=False, stop=True)
            for c in range(ST):
                ins = nc.tensor.matmul(ps[0:EXP, 3, 0:1], maskb[:, c, :], onesb[:, 0:1], start=(c == 0), stop=(c == 1))
            ins.then_inc(count_mm, 1)
            pe.wait_ge(blocks_ready, 1)
            nb = rs1[0:EXP, 11:12]
            nc.tensor.matmul(ps[0:EXP, 2, 32:33], tri, nb, start=True, stop=True)
            nc.tensor.matmul(ps[0:1, 2, 64:64 + EXP], nb, tri, start=True, stop=True).then_inc(plan_tr, 1)
            pe.wait_ge(plan_cols, 1)
            nc.tensor.matmul(ps[:, 1, 128:128 + NBC], ones[0:EXP, :], cmp, start=True, stop=True)
            nc.tensor.matmul(ps[:, 1, 192:192 + NBC], nbb, cmp, start=True, stop=True).then_inc(plan_mm, 1)

            def gather():
                for k in range(KT):
                    for c in range(ST):
                        for part in range(3):
                            ins = nc.tensor.matmul(ps[:, 3, k * BS:(k + 1) * BS], hp[:, part, c, k * P:(k + 1) * P],
                                                   onehot[:, c, :], start=(c == 0 and part == 0),
                                                   stop=(c == 1 and part == 2))
                return ins

            def scatter(last=False):
                for c in range(ST):
                    for h in range(2):
                        ins = nc.tensor.matmul(ps[:, 4 + 2 * c + h, :], selT[:, h, c * P:(c + 1) * P], ysb,
                                               start=False, stop=False, skip_group_check=True)
                        if last:
                            ins.then_inc(scattered, 1)

            pe.wait_ge(pos_ready, 1)
            for a, t in enumerate((posm, comb)):
                for c in range(ST):
                    ins = nc.tensor.transpose(ps[0:EXP, 2, (2 * a + c) * P:(2 * a + c + 1) * P], t[:, c, :], ident[:, :])
            ins.then_inc(pc_tr, 1)
            pe.wait_ge(parts, 2)
            pe.wait_ge(onehot_ready, 1)
            gather().then_inc(gather_mm, 1)
            pe.wait_ge(selT_ready, 1)
            for a in range(4):
                ins = nc.tensor.matmul(ps[:, 2, a * NBC:(a + 1) * NBC], pcT[:, a, :], bk[0:EXP, :], start=True, stop=True)
            ins.then_inc(plan_sel, 1)
            pe.wait_ge(bdown_in, 32)
            pe.wait_ge(plan, 1)
            total = pe.value_load(blk_until[0:1, EXP - 1:EXP], min_val=EXP, max_val=NBLK)

            def gate_up(e, odd, first, until):
                for k in range(first, until):
                    if k < AHEAD:
                        pe.wait_ge(gu_in[odd][k], e * 16 + 32 - 16 * odd)
                    else:
                        pe.wait_ge(gu_in[0][k], e * 16 + 16)
                    for a in range(2):
                        for h in range(2):
                            ins = nc.tensor.matmul(ps[64 * h:64 * h + 64, a, :], xT[:, k, :], gsl[odd][k][a][:, h, :],
                                                   start=False, stop=(k == KT - 1), skip_group_check=True,
                                                   tile_position=(0, 64 * h))
                    ins.then_inc(gu_done, 1)

            def down(e, odd):
                for k in range(KT):
                    pe.wait_ge(dn_in[odd][k], e * 8 + 16 - 8 * odd)
                    for h in range(2):
                        ins = nc.tensor.matmul(ps[64 * h:64 * h + 64, 2, :],
                                               actT[:, k % 4, 64 * (k // 4):64 * (k // 4) + 64],
                                               dsl[odd][k][:, h, :], start=(k == 0), stop=(k == KT - 1),
                                               skip_group_check=True, tile_position=(0, 64 * h))
                    ins.then_inc(dn_done, 1)

            def one_block(i):
                e = pe.value_load(blk_expert[0:1, bass.ds(i, 1)], min_val=0, max_val=EXP)
                odd = pe.value_load(blk_odd[0:1, bass.ds(i, 1)], min_val=0, max_val=1)
                pe.wait_ge(selT_ready, i + 1)
                for a in range(2):
                    for h in range(2):
                        nc.tensor.matmul(ps[:, a, :], ebias[0:96, h, :], bp[:, a * D + 512 * h:a * D + 512 * h + 512],
                                         start=(h == 0), stop=False, skip_group_check=True)
                pe.wait_ge(xT_ready, i + 1)
                with pe.If(odd < 1):
                    gate_up(e, 0, 0, AHEAD)
                with pe.If(odd > 0):
                    gate_up(e, 1, 0, AHEAD)
                gate_up(e, 0, AHEAD, KT)
                pe.wait_ge(y_ready, i + 1)
                scatter()
                pe.wait_ge(act_ready, i + 1)
                for j in range(4):
                    ins = nc.tensor.transpose(ps[:, 0, j * P:(j + 1) * P], l1[:, j * P:(j + 1) * P], ident[:, :])
                ins.then_inc(act_tr, 1)
                pe.wait_ge(wsel_ready, i + 1)
                for c in range(ST):
                    ins = nc.tensor.transpose(ps[:, 1, c * P:(c + 1) * P], wsel[:, c, :], ident[:, :])
                ins.then_inc(sel_tr, 1)
                pe.wait_ge(onehot_ready, i + 2)
                gather().then_inc(gather_mm, 1)
                pe.wait_ge(actT_ready, i + 1)
                with pe.If(odd < 1):
                    down(e, 0)
                with pe.If(odd > 0):
                    down(e, 1)

            with pe.Fori(0, EXP) as i:
                one_block(i)
            with pe.Fori(0, (NBLK - EXP) // TURNS) as turn:
                with pe.If(EXP + turn * TURNS < total):
                    with pe.Fori(0, TURNS) as t:
                        with pe.If(EXP + turn * TURNS + t < total):
                            one_block(EXP + turn * TURNS + t)
            pe.wait_ge(y_ready, total + 1)
            pe.wait_ge(selT_ready, total + 1)
            scatter(last=True)


_INS = ["x", "meta_tokens", "norm_mix_g", "w_in", "ssm_a_re", "ssm_a_im", "ssm_log_dt", "ssm_b_re", "ssm_b_im",
        "ssm_c_re", "ssm_c_im", "ssm_d", "w_s5_lin", "w_s5_gate", "conv_dw_w", "conv_dw_b", "conv_ln_g", "conv_ln_b",
        "w_conv_out", "w_out", "norm_ffn_g", "router_w", "router_b", "w_gate_up", "b_gate_up", "w_down", "b_down",
        "norm_final_g"]


def kernel(**inputs):
    import concourse.bacc as bacc
    from concourse.bass_utils import run_bass_kernel_spmd as run

    nc = bacc.Bacc("TRN2", target_bir_lowering=False, num_devices=1)
    arrays, aps = {}, {}
    for name in _INS:
        a = np.ascontiguousarray(inputs[name])
        arrays[f"in_{name}"] = a
        aps[name] = nc.dram_tensor(f"in_{name}", a.shape, mybir.dt.from_np(a.dtype), kind="ExternalInput").ap()
    out = nc.dram_tensor("out", (1, S, D), F32, kind="ExternalOutput").ap()
    build(nc, aps, out)
    r = run(nc, [arrays], core_ids=[0])
    return r.results[0]["out"]
```
